# Optimizing a Trainium2 kernel written in Bass

```python
import math
import jax, jax.numpy as jnp
from jax import lax
import numpy as np

D_MODEL = 2048
BATCH = 1
SEQ = 256
DEPTH = 1

CHUNK = 64

SSD_EXPAND = 2
SSD_D_INNER = SSD_EXPAND * D_MODEL
SSD_HEAD_DIM = 64
SSD_HEADS = SSD_D_INNER // SSD_HEAD_DIM
SSD_GROUPS = 8
SSD_HEADS_PER_GROUP = SSD_HEADS // SSD_GROUPS
SSD_STATE = 128
SSD_CONV = 4
SSD_CONV_DIM = SSD_D_INNER + 2 * SSD_GROUPS * SSD_STATE
SSD_NORM_GROUP = SSD_D_INNER // SSD_GROUPS

ATT_HEAD_DIM = 64
ATT_Q_HEADS = D_MODEL // ATT_HEAD_DIM
ATT_KV_HEADS = 8
ATT_GROUP = ATT_Q_HEADS // ATT_KV_HEADS
ATT_Q_WIDTH = ATT_Q_HEADS * ATT_HEAD_DIM
ATT_KV_WIDTH = ATT_KV_HEADS * ATT_HEAD_DIM
ATT_WINDOW = 128
WINDOW_CHUNKS = ATT_WINDOW // CHUNK
ATT_SCALE = ATT_HEAD_DIM ** -0.5

FFN_HIDDEN = -(-8 * D_MODEL // (3 * 256)) * 256

DEEPNORM_ALPHA = (2 * DEPTH) ** 0.25
DEEPNORM_BETA = (8 * DEPTH) ** -0.25
LN_EPS = 1e-5
RMS_EPS = 1e-5

IN_WIDTHS = (SSD_D_INNER, SSD_CONV_DIM, SSD_HEADS, ATT_Q_WIDTH, ATT_KV_WIDTH, ATT_KV_WIDTH, D_MODEL, D_MODEL)
IN_SPLITS = tuple(int(s) for s in np.cumsum(IN_WIDTHS)[:-1])
N_IN = int(sum(IN_WIDTHS))

kernel_name = "hybrid_ssd_swa_sink_gated_deepnorm"

F32 = jnp.float32

def layer_norm(x, g, b):
    xf = x.astype(F32)
    mu = jnp.mean(xf, axis=-1, keepdims=True)
    xc = xf - mu
    var = jnp.mean(xc * xc, axis=-1, keepdims=True)
    return (xc * lax.rsqrt(var + LN_EPS) * g + b).astype(x.dtype)

def causal_depthwise_conv(u, w, bias):
    k_taps = w.shape[0]
    seq = u.shape[1]
    up = jnp.pad(u, ((0, 0), (k_taps - 1, 0), (0, 0)))
    out = bias + w[0] * up[:, 0:seq]
    for k in range(1, k_taps):
        out = out + w[k] * up[:, k:k + seq]
    return out

def shift_chunks(t, j):
    if j == 0:
        return t
    nc = t.shape[1]
    pad = [(0, 0), (j, 0)] + [(0, 0)] * (t.ndim - 2)
    return jnp.pad(t, pad)[:, :nc]

def ssd_chunked(xh, dt, a, bm, cm):
    b, seq = xh.shape[0], xh.shape[1]
    nc = seq // CHUNK
    G, R, P, N = SSD_GROUPS, SSD_HEADS_PER_GROUP, SSD_HEAD_DIM, SSD_STATE
    x = (xh * dt[..., None]).reshape(b, nc, CHUNK, G, R, P)
    da = jnp.transpose((dt * a).reshape(b, nc, CHUNK, G, R), (0, 3, 4, 1, 2))
    a_cum = jnp.cumsum(da, axis=-1)
    B = bm.reshape(b, nc, CHUNK, G, N)
    C = cm.reshape(b, nc, CHUNK, G, N)

    seg = a_cum[..., :, None] - a_cum[..., None, :]
    causal = jnp.tril(jnp.ones((CHUNK, CHUNK), dtype=bool))
    decay = jnp.exp(jnp.where(causal, seg, -jnp.inf))
    cb = jnp.einsum('bclgn,bcsgn->bgcls', C, B)
    w = cb[:, :, None] * decay
    y_diag = jnp.einsum('bgrcls,bcsgrp->bclgrp', w, x)

    decay_to_end = jnp.transpose(jnp.exp(a_cum[..., -1:] - a_cum), (0, 3, 4, 1, 2))
    states = jnp.einsum('bclgn,bclgrp->cbgrpn', B, x * decay_to_end[..., None])

    chunk_decay = jnp.moveaxis(jnp.exp(a_cum[..., -1]), -1, 0)

    def step(h, inp):
        s_c, d_c = inp
        return d_c[..., None, None] * h + s_c, h

    h0 = jnp.zeros((b, G, R, P, N), F32)
    _, prev = lax.scan(step, h0, (states, chunk_decay))

    decay_in = jnp.transpose(jnp.exp(a_cum), (0, 3, 4, 1, 2))
    y_off = jnp.einsum('bclgn,cbgrpn->bclgrp', C, prev) * decay_in[..., None]
    return (y_diag + y_off).reshape(b, seq, SSD_HEADS, P)

def sliding_window_sink_attention(q, k, v, sinks):
    b, seq = q.shape[0], q.shape[1]
    nc = seq // CHUNK
    q = q.reshape(b, nc, CHUNK, ATT_KV_HEADS, ATT_GROUP, ATT_HEAD_DIM)
    k = k.reshape(b, nc, CHUNK, ATT_KV_HEADS, ATT_HEAD_DIM)
    v = v.reshape(b, nc, CHUNK, ATT_KV_HEADS, ATT_HEAD_DIM)
    back_order = range(WINDOW_CHUNKS - 1, -1, -1)
    k_band = jnp.concatenate([shift_chunks(k, j) for j in back_order], axis=2)
    v_band = jnp.concatenate([shift_chunks(v, j) for j in back_order], axis=2)
    s = jnp.einsum('bclkgd,bcskd->bkgcls', q, k_band).astype(F32) * ATT_SCALE
    back = (WINDOW_CHUNKS - 1) - jnp.arange(WINDOW_CHUNKS * CHUNK) // CHUNK
    valid = jnp.arange(nc)[:, None] >= back[None, :]
    s = jnp.where(valid[:, None, :], s, -jnp.inf)
    sink = sinks.astype(F32).reshape(ATT_KV_HEADS, ATT_GROUP)[None, :, :, None, None, None]
    sink = jnp.broadcast_to(sink, s.shape[:-1] + (1,))
    p = jax.nn.softmax(jnp.concatenate([s, sink], axis=-1), axis=-1)[..., :-1]
    o = jnp.einsum('bkgcls,bcskd->bclkgd', p.astype(v.dtype), v_band)
    return o.reshape(b, seq, ATT_Q_WIDTH)

def token_mixer(x, w_in, conv_w, conv_b, dt_bias, a_log, d_skip, ssd_norm_w, sinks, w_pa, w_pb, w_o):
    b, seq, _ = x.shape
    proj = x @ w_in
    z, xbc, dt, q, k, v, ga, gb = jnp.split(proj, IN_SPLITS, axis=-1)

    xbc = jax.nn.silu(causal_depthwise_conv(xbc, conv_w, conv_b))
    xs, bm, cm = jnp.split(xbc, (SSD_D_INNER, SSD_D_INNER + SSD_GROUPS * SSD_STATE), axis=-1)
    dt = jax.nn.softplus(dt.astype(F32) + dt_bias.astype(F32))
    a = -jnp.exp(a_log.astype(F32))
    xh = xs.reshape(b, seq, SSD_HEADS, SSD_HEAD_DIM).astype(F32)
    y = ssd_chunked(xh, dt, a,
                    bm.reshape(b, seq, SSD_GROUPS, SSD_STATE).astype(F32),
                    cm.reshape(b, seq, SSD_GROUPS, SSD_STATE).astype(F32))
    y = y + d_skip.astype(F32)[:, None] * xh
    y = y.reshape(b, seq, SSD_D_INNER) * jax.nn.silu(z.astype(F32))
    yg = y.reshape(b, seq, SSD_GROUPS, SSD_NORM_GROUP)
    yg = yg * lax.rsqrt(jnp.mean(yg * yg, axis=-1, keepdims=True) + RMS_EPS)
    y_ssd = (yg.reshape(b, seq, SSD_D_INNER) * ssd_norm_w).astype(x.dtype)

    y_att = sliding_window_sink_attention(q, k, v, sinks)

    merged = jax.nn.sigmoid(ga) * (y_ssd @ w_pa) + jax.nn.sigmoid(gb) * (y_att @ w_pb)
    return merged @ w_o

def swiglu(x, w_gu, w_down):
    gate, up = jnp.split(x @ w_gu, 2, axis=-1)
    return (jax.nn.silu(gate) * up) @ w_down

def setup_inputs(seed: int = 0) -> dict:
    key = jax.random.key(seed)
    ks = jax.random.split(key, 24)

    def nrm(k, shape, scale):
        return jax.random.normal(k, shape, F32) * scale

    x = jax.random.normal(ks[0], (BATCH, SEQ, D_MODEL), F32)
    w_in = nrm(ks[1], (DEPTH, D_MODEL, N_IN), D_MODEL ** -0.5)
    conv_w = nrm(ks[2], (DEPTH, SSD_CONV, SSD_CONV_DIM), SSD_CONV ** -0.5)
    conv_b = nrm(ks[3], (DEPTH, SSD_CONV_DIM), 0.02)
    dt0 = jnp.exp(jax.random.uniform(ks[4], (DEPTH, SSD_HEADS), F32, math.log(1e-3), math.log(1e-1)))
    dt_bias = dt0 + jnp.log(-jnp.expm1(-dt0))
    a_log = jnp.log(jax.random.uniform(ks[5], (DEPTH, SSD_HEADS), F32, 1.0, 16.0))
    d_skip = 1.0 + nrm(ks[6], (DEPTH, SSD_HEADS), 0.02)
    ssd_norm_w = 1.0 + nrm(ks[7], (DEPTH, SSD_D_INNER), 0.02)
    sinks = nrm(ks[8], (DEPTH, ATT_Q_HEADS), 1.0)
    w_pa = nrm(ks[9], (DEPTH, SSD_D_INNER, D_MODEL), SSD_D_INNER ** -0.5)
    w_pb = nrm(ks[10], (DEPTH, ATT_Q_WIDTH, D_MODEL), ATT_Q_WIDTH ** -0.5)
    w_o = nrm(ks[11], (DEPTH, D_MODEL, D_MODEL), DEEPNORM_BETA * D_MODEL ** -0.5)
    ln1_g = 1.0 + nrm(ks[12], (DEPTH, D_MODEL), 0.02)
    ln1_b = nrm(ks[13], (DEPTH, D_MODEL), 0.02)
    w_gu = nrm(ks[14], (DEPTH, D_MODEL, 2 * FFN_HIDDEN), D_MODEL ** -0.5)
    w_down = nrm(ks[15], (DEPTH, FFN_HIDDEN, D_MODEL), DEEPNORM_BETA * FFN_HIDDEN ** -0.5)
    ln2_g = 1.0 + nrm(ks[16], (DEPTH, D_MODEL), 0.02)
    ln2_b = nrm(ks[17], (DEPTH, D_MODEL), 0.02)
    return {"x": x, "w_in": w_in, "conv_w": conv_w, "conv_b": conv_b, "dt_bias": dt_bias,
            "a_log": a_log, "d_skip": d_skip, "ssd_norm_w": ssd_norm_w, "sinks": sinks,
            "w_pa": w_pa, "w_pb": w_pb, "w_o": w_o, "ln1_g": ln1_g, "ln1_b": ln1_b,
            "w_gu": w_gu, "w_down": w_down, "ln2_g": ln2_g, "ln2_b": ln2_b}

def reference(x, w_in, conv_w, conv_b, dt_bias, a_log, d_skip, ssd_norm_w, sinks,
              w_pa, w_pb, w_o, ln1_g, ln1_b, w_gu, w_down, ln2_g, ln2_b):
    for i in range(DEPTH):
        h = token_mixer(x, w_in[i], conv_w[i], conv_b[i], dt_bias[i], a_log[i], d_skip[i],
                        ssd_norm_w[i], sinks[i], w_pa[i], w_pb[i], w_o[i])
        x = layer_norm(DEEPNORM_ALPHA * x + h, ln1_g[i], ln1_b[i])
        x = layer_norm(DEEPNORM_ALPHA * x + swiglu(x, w_gu[i], w_down[i]), ln2_g[i], ln2_b[i])
    return x


_drawn_inputs = setup_inputs


def setup_inputs(seed=0):
    import zlib

    import numpy as np

    out = dict(_drawn_inputs(seed))
    spreads = {}
    factors = {'conv_b': 7.481,
     'd_skip': 8.0,
     'ssd_norm_w': 8.0,
     'sinks': 56.905,
     'ln1_g': 2.783,
     'ln1_b': 2.667,
     'ln2_g': 8.444,
     'ln2_b': 8.216,
     'w_pb': 2.898}
    for name, (base, spread) in spreads.items():
        noise = np.random.default_rng([zlib.crc32(name.encode()), seed]).standard_normal(out[name].shape)
        drawn = base * np.exp(spread * noise) if base else spread * noise
        out[name] = __import__('jax').numpy.asarray(drawn.astype(out[name].dtype))
    for name, factor in factors.items():
        out[name] = (out[name] * factor).astype(out[name].dtype)
    return out
```

```python
from contextlib import ExitStack

import numpy as np
import concourse.bass as bass
from concourse import mybir

F32 = mybir.dt.float32
F32R = mybir.dt.float32r
ACT = mybir.ActivationFunctionType
ALU = mybir.AluOpType
AX = mybir.AxisListType

P = 128
D_MODEL = 2048
SEQ = 256
SSD_INNER = 2 * D_MODEL
SSD_HEADS = 64
SSD_GROUPS = 8
HEADS_PER_GROUP = SSD_HEADS // SSD_GROUPS
SSD_STATE = 128
SSD_HEAD_DIM = 64
CONV_TAPS = 4
CONV_DIM = SSD_INNER + 2 * SSD_GROUPS * SSD_STATE
Q_HEADS = 32
KV_HEADS = 8
ATT_HEAD_DIM = 64
ATT_CHUNK = 64
KV_WIDTH = KV_HEADS * ATT_HEAD_DIM
FFN_HIDDEN = -(-8 * D_MODEL // (3 * 256)) * 256
ALPHA = 2 ** 0.25
ATT_SCALE = ATT_HEAD_DIM ** -0.5
LN_EPS = 1e-5
RMS_EPS = 1e-5

Z_COL = 0
XS_COL = SSD_INNER
B_COL = XS_COL + SSD_INNER
C_COL = B_COL + SSD_GROUPS * SSD_STATE
DT_COL = Z_COL + SSD_INNER + CONV_DIM
Q_COL = DT_COL + SSD_HEADS
K_COL = Q_COL + Q_HEADS * ATT_HEAD_DIM
V_COL = K_COL + KV_WIDTH
GA_COL = V_COL + KV_WIDTH
GB_COL = GA_COL + D_MODEL

RING = 4
CHUNK = 1024
KT = D_MODEL // P
KT_Y = SSD_INNER // P
KT_H = FFN_HIDDEN // P
GU_PAIRS = FFN_HIDDEN // 256

Y_TILE = [12, 16, 0, 4, 8, 20, 24, 28]

C_KV, B_KV = 0, 0
C_ATT, B_ATT = 16, 4
C_DT, B_DT = C_ATT + 8 * KV_HEADS, B_ATT + 2 * KV_HEADS
C_PB, B_PB = C_DT + 2, B_DT + 1
C_SSD, B_SSD = C_PB + 32, B_PB + 8
C_PA, B_PA = C_SSD + 24 * SSD_GROUPS, B_SSD + 6 * SSD_GROUPS
C_O, B_O = C_PA + 64, B_PA + 8
C_GU, B_GU = C_O + 32, B_O + 8
C_DN, B_DN = C_GU + 8 * GU_PAIRS, B_GU + 2 * GU_PAIRS

K_ID, K_ONES, K_CUM0, K_CUM1, K_CAUSAL, K_BAND = 0, 128, 256, 384, 512, 896
K_WIDTH = 1280
GP_CONV, GP_BIAS, GP_SKIP, GP_NORM = 0, 24, 30, 34
GP_WIDTH = 38
LN_COL = SSD_GROUPS * GP_WIDTH
PAR_WIDTH = LN_COL + 4 * KT


class Count:

    def __init__(self, base, step=0, i=None):
        self.base, self.step, self.i = base, step, i

    def __add__(self, n):
        return Count(self.base + n, self.step, self.i)

    def value(self):
        return self.base if self.i is None else self.i * self.step + self.base


def at(i, base, step):
    return Count(base + step * i) if isinstance(i, int) else Count(base, step, i)


def wait(eng, sem, count):
    count = count if isinstance(count, Count) else Count(count)
    if count.i is None and count.base <= 0:
        return
    eng.wait_ge(sem, count.value())


class Chain:

    def __init__(self, eng, sem):
        self.eng, self.sem, self.total, self.loop = eng, sem, 0, None

    def mark(self, ins):
        ins.then_inc(self.sem, 1)
        self.total += 1

    def wait(self):
        if self.loop is None:
            self.eng.wait_ge(self.sem, self.total)
        else:
            i, first, per, entry = self.loop
            self.eng.wait_ge(self.sem, i * per + (self.total - first * per))

    def link(self, ins):
        self.mark(ins)
        self.wait()

    def enter(self, i, first, per):
        self.loop = (i, first, per, self.total)

    def leave(self, times):
        i, first, per, entry = self.loop
        assert self.total - entry == per, self.total - entry
        self.total = entry + per * times
        self.loop = None


def ds(i, step, base, size):
    if isinstance(i, int):
        return slice(i * step + base, i * step + base + size)
    return bass.ds(i * step + base, size)


def hybrid_trunk(nc, x_t, w_in, heads, sinks, w_pa, w_pb, w_o, w_gu, w_down, consts, params, out_t):
    with ExitStack() as ctx:
        def sem(name):
            return ctx.enter_context(nc.semaphore(name))

        KB = 1024
        arena = (nc.sbuf_base + 63) // 64 * 64
        place = [arena]

        def put(name, shape, dtype, offset=None):
            size = 4
            for n in shape[1:]:
                size *= n
            if offset is None:
                offset = place[0]
                place[0] += (size + 31) // 32 * 32
            assert offset + size <= nc.sbuf_usable_end, (name, offset + size)
            return nc.alloc_sbuf_tensor_at(name, shape, dtype, offset=offset)

        raw = put("raw", [P, RING, CHUNK], F32)
        w_hi = put("w_hi", [P, RING, CHUNK], F32R)
        w_lo = put("w_lo", [P, RING, CHUNK], F32R)
        low = put("low", [P, 2, 2, SEQ], F32)
        cst = put("cst", [P, K_WIDTH], F32)
        par = put("par", [P, PAR_WIDTH], F32)
        sink_b = put("sink_b", [P, Q_HEADS], F32)
        hd = put("hd", [SSD_HEADS, 2], F32)
        x_at = place[0]
        x_hl = put("x_hl", [P, KT, 2, SEQ], F32R)
        x1_hl = put("x1_hl", [P, KT, 2, SEQ], F32R, x_at)
        g_at = place[0]
        gates = put("gates", [P, KT, 2, SEQ], F32)
        merged_hl = put("merged_hl", [P, KT, 2, SEQ], F32R, g_at)
        w_at = place[0]
        h_hl = put("h_hl", [P, KT_H, 2, SEQ], F32R, g_at)

        yatt_hl = put("yatt_hl", [P, KT, 2, SEQ], F32R, w_at)
        place[0] = w_at + 32 * KB
        x_raw = put("x_raw", [P, KT, SEQ], F32)
        kd = put("kd", [P, KV_HEADS, SEQ], F32)
        kz = put("kz", [P, 2, SEQ], F32)
        v_tm = put("v_tm", [P, 2, KV_WIDTH], F32)
        v_cur = put("v_cur", [P, 2, ATT_HEAD_DIM], F32)
        q_fm = put("q_fm", [P, 2, SEQ], F32)
        prob = put("prob", [P, 4, 384], F32, place[0])
        kv_fm = put("kv_fm", [P, 8, SEQ], F32, w_at)
        place[0] += 6 * KB
        prob_t = put("prob_t", [P, 12, P], F32)
        o_tm = put("o_tm", [P, 8, ATT_HEAD_DIM], F32)
        peak = put("peak", [P, 2, 4], F32)
        sink_d = put("sink_d", [P, 2, 4], F32)
        denom = put("denom", [P, 2, 4], F32)
        recip = put("recip", [P, 2, 4], F32)

        y_plain = put("y_plain", [P, KT_Y, SEQ], F32, w_at)
        y_lo = put("y_lo", [P, KT_Y, SEQ], F32R, w_at)
        y_hi = put("y_hi", [P, KT_Y, SEQ], F32R, w_at + 32 * KB)
        place[0] = w_at + 32 * KB
        weights = put("weights", [P, HEADS_PER_GROUP, 384], F32)
        c_row = put("c_row", [P, HEADS_PER_GROUP, SEQ], F32)
        x_dt = put("x_dt", [P, 2, HEADS_PER_GROUP * SSD_HEAD_DIM], F32)
        square = put("square", [P, 4, SEQ], F32)
        conv_in = put("conv_in", [P, 2, SEQ + 4], F32)
        cb = put("cb", [P, 384], F32)
        place[0] = max(place[0], w_at + 64 * KB)
        xc = put("xc", [P, 6, SEQ], F32)
        zc = put("zc", [P, 4, SEQ], F32)
        stat = put("stat", [P, SEQ], F32)
        rstd = put("rstd", [P, SEQ], F32)
        tmp = put("tmp", [P, 2, SEQ], F32)
        dt_tm = put("dt_tm", [P, 2, SSD_HEADS], F32)
        ncum = put("ncum", [P, 2, SSD_HEADS], F32)
        ncum_g = put("ncum_g", [P, 2, HEADS_PER_GROUP], F32)
        dt_g = put("dt_g", [P, 2, HEADS_PER_GROUP], F32)
        gp = put("gp", [P, GP_WIDTH], F32)
        dts = [put(f"dts{n}", [SSD_HEADS, SEQ], F32, w_at + 32 * KB + n * KB) for n in range(7)]
        da_tm = put("da_tm", [P, 2, SSD_HEADS], F32, w_at + 39 * KB)
        neg_a = put("neg_a", [SSD_HEADS, 1], F32, w_at + 40 * KB)

        f_at = g_at + KT_H * 2 * KB
        assert f_at >= w_at + 56 * KB - 64
        place[0] = f_at
        res = put("res", [P, KT, SEQ], F32)
        acc = put("acc", [P, SEQ], F32)
        t2 = put("t2", [P, 2, SEQ], F32)
        sq2 = put("sq2", [P, 2, 2, SEQ], F32, place[0])
        gate_g = put("gate_g", [P, 2, SEQ], F32)
        place[0] += 2 * KB
        mean = put("mean", [P, SEQ], F32)
        lstat = put("lstat", [P, SEQ], F32)
        lrstd = put("lrstd", [P, SEQ], F32)

        ident = cst[:, K_ID:K_ID + P]
        ones = cst[:, K_ONES:K_ONES + P]
        cum = [cst[:, K_CUM0:K_CUM0 + P], cst[:, K_CUM1:K_CUM1 + P]]
        causal = cst[:, K_CAUSAL:K_CAUSAL + 384]
        band = cst[:, K_BAND:K_BAND + 384]

        ps = ctx.enter_context(nc.psum_tensor("ps", [P, 4, 2, SEQ], F32))
        pw = ctx.enter_context(nc.psum_tensor("pw", [P, 4, 512], F32))

        c_rows = nc.dram_tensor("c_rows", (SSD_GROUPS, HEADS_PER_GROUP * SEQ), F32, kind="Internal").ap()

        x_landed = [sem(f"x_landed{n}") for n in range(4)]
        consts_landed = sem("consts_landed")
        raw_landed = [sem(f"raw_landed{n}") for n in range(RING)]
        hi_split = sem("hi_split")
        lo_split = sem("lo_split")
        chunk_multiplied = sem("chunk_multiplied")
        low_copied = sem("low_copied")
        block_evacuated = sem("block_evacuated")
        x_hi_done, x_lo_done = sem("x_hi_done"), sem("x_lo_done")
        k_spread, v_turned, v_ready = sem("k_spread"), sem("v_turned"), sem("v_ready")
        k_picked, v_picked = sem("k_picked"), sem("v_picked")
        scores_done, shifted, exp_done = sem("scores_done"), sem("shifted"), sem("exp_done")
        probs_turned, probs_copied = sem("probs_turned"), sem("probs_copied")
        att_done, att_scaled, att_turned = sem("att_done"), sem("att_scaled"), sem("att_turned")
        yatt_hi_done, yatt_lo_done = sem("yatt_hi_done"), sem("yatt_lo_done")
        merged_part = sem("merged_part")
        gb_sigmoid, ga_sigmoid = sem("gb_sigmoid"), sem("ga_sigmoid")
        dt_neg_abs, dt_exp, dt_ready, dt_turned = sem("dt_neg_abs"), sem("dt_exp"), sem("dt_ready"), sem("dt_turned")
        dt_copied, cum_done, cum_copied, cum_stored = sem("dt_copied"), sem("cum_done"), sem("cum_copied"), sem("cum_stored")
        neg_cum_ready = sem("neg_cum_ready")
        c_row_landed = sem("c_row_landed")
        seg_ready, decay_done = sem("seg_ready"), sem("decay_done")
        conv_done, conv_silu_done, z_silu_done = sem("conv_done"), sem("conv_silu_done"), sem("z_silu_done")
        xt_done, x_dt_ready = sem("xt_done"), sem("x_dt_ready")
        weights_ready, y_done = sem("weights_ready"), sem("y_done")
        gated, squared, square_summed = sem("gated"), sem("squared"), sem("square_summed")
        norm_summed, var_ready, sqrt_done, y_ready = sem("norm_summed"), sem("var_ready"), sem("sqrt_done"), sem("y_ready")
        y_hi_done, y_lo_done = sem("y_hi_done"), sem("y_lo_done")
        merged_ready, merged_hi_done, merged_lo_done = sem("merged_ready"), sem("merged_hi_done"), sem("merged_lo_done")
        ln_acc_ready, ln_mean_done, ln_centred = sem("ln_acc_ready"), sem("ln_mean_done"), sem("ln_centred")
        ln_squared, ln_sq_summed, ln_var_ready = sem("ln_squared"), sem("ln_sq_summed"), sem("ln_var_ready")
        ln_sqrt_done, ln_scaled = sem("ln_sqrt_done"), sem("ln_scaled")
        x1_hi_done, x1_lo_done = sem("x1_hi_done"), sem("x1_lo_done")
        gate_silu, h_taken, h_hi_done, h_lo_done = (
            sem("gate_silu"), sem("h_taken"), sem("h_hi_done"), sem("h_lo_done"))
        out_ready, out_stored = sem("out_ready"), sem("out_stored")
        dve_step = sem("dve_step")

        block = ctx.enter_context(nc.Block())

        @block.sync
        def _(sp):
            def load(c, src):
                wait(sp, lo_split, c + (1 - RING))
                slot = c.base % RING
                n = src.shape[2]
                sp.dma_start(raw[:, slot, :].rearrange("p (k n) -> p k n", n=n), src).then_inc(raw_landed[slot], 16)

            def wide(w, kc, cols):
                return w[kc * 512:(kc + 1) * 512, cols].rearrange("(k p) n -> p k n", p=P)

            def tall(w, kc, cols):
                return w[kc * 1024:(kc + 1) * 1024, cols].rearrange("(k p) n -> p k n", p=P)

            def load_block(c, w, cols, n):
                for kc in range(n):
                    load(c + kc, wide(w, kc, cols))

            for n in range(4):
                for kc in range(4):
                    if n == 0:
                        sp.dma_start(x_raw[:, 4 * kc:4 * kc + 4, :], x_t[512 * kc:512 * kc + 512].rearrange(
                            "(k p) t -> p k t", p=P)).then_inc(x_landed[kc], 16)
                    load(Count(C_KV + 4 * n + kc), wide(w_in, kc, slice(K_COL + 256 * n, K_COL + 256 * (n + 1))))

            with sp.Fori(0, KV_HEADS) as j:
                c = at(j, C_ATT, 8)
                load_block(c, w_in, ds(j, 256, Q_COL, 256), 4)
                load_block(c + 4, w_in, ds(j, 256, GB_COL, 256), 4)

            for kc in range(2):
                load(Count(C_DT + kc), tall(w_in, kc, slice(DT_COL, DT_COL + P)))

            with sp.Fori(0, 4) as i:
                for b in range(2):
                    load_block(at(i, C_PB + 4 * b, 8), w_pb, ds(i, 512, 256 * b, 256), 4)

            with sp.Fori(0, SSD_GROUPS) as g:
                c = at(g, C_SSD, 24)
                for b in range(2):
                    load_block(c + 4 * b, w_in, ds(g, 512, XS_COL + 256 * b, 256), 4)
                for kc in range(2):
                    load(c + (8 + kc), tall(w_in, kc, ds(g, P, B_COL, P)))
                for kc in range(2):
                    load(c + (10 + kc), tall(w_in, kc, ds(g, P, C_COL, P)))
                for b in range(2):
                    load_block(c + (12 + 4 * b), w_in, bass.ds((g * 256) * 2 + (Z_COL + 256 * b), 256), 4)
                load_block(c + 20, w_in, ds(g, 256, GA_COL, 256), 4)

            with sp.Fori(0, 4) as i:
                for b in range(2):
                    load_block(at(i, C_PA + 8 * b, 16), w_pa, ds(i, 512, 256 * b, 256), 8)

            with sp.Fori(0, 4) as i:
                for b in range(2):
                    load_block(at(i, C_O + 4 * b, 8), w_o, ds(i, 512, 256 * b, 256), 4)

            with sp.Fori(0, GU_PAIRS) as i:
                load_block(at(i, C_GU, 8), w_gu, ds(i, 256, 0, 256), 4)
                load_block(at(i, C_GU + 4, 8), w_gu, ds(i, 256, FFN_HIDDEN, 256), 4)

            with sp.Fori(0, 2) as i:
                for b in range(4):
                    load_block(at(i, C_DN + 11 * b, 44), w_down, ds(i, 1024, 256 * b, 256), 11)

            out_v = out_t.rearrange("(k p) t -> p k t", p=P)
            for n in range(4):
                sp.wait_ge(out_ready, 4 * (n + 1))
                sp.dma_start(out_v[:, 4 * n:4 * n + 4, :], res[:, 4 * n:4 * n + 4, :]).then_inc(out_stored, 16)
            sp.wait_ge(out_stored, 64)

        @block.gpsimd
        def _(pool):
            pool.dma_start(cst[:], consts).then_inc(consts_landed, 16)
            pool.dma_start(par[:], params).then_inc(consts_landed, 16)
            pool.dma_start(sink_b[:], sinks.to_broadcast([P, Q_HEADS])).then_inc(consts_landed, 16)
            pool.dma_start(hd[:], heads).then_inc(consts_landed, 16)
            pool.wait_ge(block_evacuated, B_KV + 2)
            for half in range(2):
                for odd in range(2):
                    dst = kd[64 * half:64 * half + 64].rearrange("p (a b) t -> p b a t", b=2)[:, odd]
                    pool.dma_start(dst, kv_fm[64 * odd:64 * odd + 64, 0:4, :]).then_inc(k_spread, 16)
            pool.wait_ge(cum_copied, 1)
            pool.dma_start(c_rows.rearrange("g (h t) -> (g h) t", h=HEADS_PER_GROUP), dts[0][:]).then_inc(cum_stored, 16)
            pool.wait_ge(cum_stored, 16)

            def spread_rows(g):
                pool.dma_start(c_row[:].rearrange("p h t -> p (h t)"),
                               c_rows[ds(g, 1, 0, 1), :].to_broadcast([P, HEADS_PER_GROUP * SEQ])
                               ).then_inc(c_row_landed, 16)

            spread_rows(0)
            with pool.Fori(1, SSD_GROUPS) as g:
                wait(pool, seg_ready, at(g, 0, 2))
                spread_rows(g)

        @block.tensor
        def _(pe):
            def multiply(c, b, wide, pair, kts, rhs_hi, rhs_lo, rhs_hl, first, last):
                wait(pe, lo_split, c + 1)
                if first:
                    wait(pe, block_evacuated, b + (-1))
                slot = c.base % RING
                mm = None
                for m in pair:
                    bank = 2 * (b.base % 2) + m
                    for n, kt in enumerate(kts):
                        o = n * 256 + m * P if wide else n * P
                        start = first and n == 0
                        if rhs_hl is not None:
                            pe.matmul(ps[:, bank, :, :], w_hi[:, slot, o:o + P], rhs_hl(kt),
                                      start=start, stop=False, skip_group_check=True)
                        else:
                            pe.matmul(ps[:, bank, 0, :], w_hi[:, slot, o:o + P], rhs_hi(kt),
                                      start=start, stop=False, skip_group_check=True)
                            pe.matmul(ps[:, bank, 1, :], w_hi[:, slot, o:o + P], rhs_lo(kt),
                                      start=False, stop=False, skip_group_check=True)
                        mm = pe.matmul(ps[:, bank, 1, :], w_lo[:, slot, o:o + P], rhs_hi(kt),
                                       start=False, stop=last and n == len(kts) - 1, skip_group_check=True)
                mm.then_inc(chunk_multiplied, 1)

            def hl(buf):
                return dict(rhs_hi=lambda kt: buf[:, kt, 0, :], rhs_lo=None, rhs_hl=lambda kt: buf[:, kt, :, :])

            X, YA, M, X1, H = hl(x_hl), hl(yatt_hl), hl(merged_hl), hl(x1_hl), hl(h_hl)
            Y = dict(rhs_hi=lambda kt: y_hi[:, Y_TILE[kt // 4] + kt % 4, :], rhs_lo=lambda kt: y_lo[:, kt, :], rhs_hl=None)

            def wide(c, b, kc, n, src):
                multiply(c + kc, b, True, (0, 1), range(4 * kc, 4 * kc + 4), first=kc == 0, last=kc == n - 1, **src)

            def tall(c, b, kc, m, src):
                multiply(c + kc, b, False, (m,), range(8 * kc, 8 * kc + 8), first=kc == 0, last=kc == 1, **src)

            def turn(out, in_):
                return pe.transpose(out, in_, ident)

            for n in range(4):
                for kc in range(4):
                    if n == 0:
                        pe.wait_ge(x_lo_done, kc + 1)
                    wide(Count(C_KV + 4 * n), Count(B_KV + n), kc, 4, X)

            def att_scores(j):
                wait(pe, block_evacuated, at(j, B_ATT + 1, 2))
                wait(pe, k_picked, at(j, 1, 1))
                for h in range(4):
                    kk = kz[:, h % 2, :]
                    pe.matmul(pw[:, 0, P * h:P * h + P], q_fm[:, h // 2, 0:P], kk[:, 0:P],
                              start=True, stop=True, skip_group_check=True)
                    mm = pe.matmul(pw[:, 1 + h // 2, 256 * (h % 2):256 * (h % 2) + 256], q_fm[:, h // 2, P:2 * P], kk,
                                   start=True, stop=True, skip_group_check=True)
                mm.then_inc(scores_done, 1)

            def att_turn_probs(j):
                wait(pe, exp_done, at(j, 1, 1))
                for n in range(12):
                    mm = turn(pw[:, n // 4, P * (n % 4):P * (n % 4) + P], prob[:, n // 3, P * (n % 3):P * (n % 3) + P])
                mm.then_inc(probs_turned, 1)

            def att_values(j):
                wait(pe, probs_copied, at(j, 1, 1))
                wait(pe, v_picked, at(j, 1, 1))
                for h in range(4):
                    o = ATT_HEAD_DIM * h
                    pe.matmul(pw[:, 3, o:o + 64], prob_t[:, 3 * h, :], v_cur[:, 0, :],
                              start=True, stop=True, skip_group_check=True)
                    pe.matmul(pw[:, 3, 256 + o:256 + o + 64], prob_t[:, 3 * h + 1, :], v_cur[:, 0, :],
                              start=True, stop=False, skip_group_check=True)
                    mm = pe.matmul(pw[:, 3, 256 + o:256 + o + 64], prob_t[:, 3 * h + 2, :], v_cur[:, 1, :],
                                   start=False, stop=True, skip_group_check=True)
                mm.then_inc(att_done, 1)

            def att_turn_out(j):
                wait(pe, att_scaled, at(j, 1, 1))
                for f in range(2):
                    for t in range(2):
                        mm = turn(pw[:, 3, 256 * f + P * t:256 * f + P * t + P],
                                  o_tm[:, 4 * t + 2 * f:4 * t + 2 * f + 2, :].rearrange("p h d -> p (h d)"))
                mm.then_inc(att_turned, 1)

            pe.wait_ge(consts_landed, 64)

            def attention(j, first=False):
                c, b = at(j, C_ATT, 8), at(j, B_ATT, 2)
                before = j - 1
                for kc in range(3):
                    wide(c, b, kc, 4, X)
                if not first:
                    att_turn_probs(before)
                wide(c, b, 3, 4, X)
                if first:
                    pe.wait_ge(block_evacuated, B_KV + 4)
                    for f in range(4):
                        for t in range(2):
                            mm = turn(pw[:, t, P * f:P * f + P], kv_fm[:, 4 + f, P * t:P * t + P])
                    mm.then_inc(v_turned, 1)
                else:
                    att_values(before)
                wide(c + 4, b + 1, 0, 4, X)
                if not first:
                    att_turn_out(before)
                wide(c + 4, b + 1, 1, 4, X)
                if first:
                    pe.wait_ge(v_ready, 1)
                att_scores(j)
                for kc in range(2, 4):
                    wide(c + 4, b + 1, kc, 4, X)

            attention(0, first=True)
            with pe.Fori(1, KV_HEADS) as j:
                attention(j)

            for kc in range(2):
                tall(Count(C_DT), Count(B_DT), kc, 0, X)
            tail = KV_HEADS - 1
            c, b = Count(C_PB), Count(B_PB)
            pe.wait_ge(yatt_lo_done, tail)
            wide(c, b, 0, 4, YA)
            att_turn_probs(tail)
            wide(c, b, 1, 4, YA)
            att_values(tail)
            wide(c, b, 2, 4, YA)
            att_turn_out(tail)
            pe.wait_ge(yatt_lo_done, KV_HEADS)
            wide(c, b, 3, 4, YA)
            for kc in range(4):
                wide(c + 4, b + 1, kc, 4, YA)
            with pe.Fori(1, 3) as i:
                for n in range(2):
                    for kc in range(4):
                        wide(at(i, C_PB + 4 * n, 8), at(i, B_PB + n, 2), kc, 4, YA)
            c, b = Count(C_PB + 24), Count(B_PB + 6)
            wide(c, b, 0, 4, YA)
            pe.wait_ge(dt_ready, 1)
            for t in range(2):
                pe.transpose(pw[:, 0, 64 * t:64 * t + 64], dts[5][:, P * t:P * t + P], cst[0:64, K_ID:K_ID + 64])
                mm = pe.transpose(pw[:, 0, P + 64 * t:P + 64 * t + 64], dts[6][:, P * t:P * t + P], cst[0:64, K_ID:K_ID + 64])
            mm.then_inc(dt_turned, 1)
            for kc in range(1, 4):
                wide(c, b, kc, 4, YA)
            pe.wait_ge(dt_copied, 1)
            for t in range(2):
                pe.matmul(pw[:, 1, 64 * t:64 * t + 64], cum[t], da_tm[:, t, :], start=True, stop=True,
                          skip_group_check=True)
                mm = pe.matmul(pw[0:64, 2, P * t:P * t + P], da_tm[:, t, :], cum[t], start=True, stop=True,
                               skip_group_check=True)
            mm.then_inc(cum_done, 1)
            for kc in range(4):
                wide(c + 4, b + 1, kc, 4, YA)

            def ssd_turn_x(g):
                wait(pe, conv_silu_done, at(g, 3, 3))
                for f in range(4):
                    for t in range(2):
                        turn(pw[:, t, P * f:P * f + P], xc[:, f, P * t:P * t + P])
                pe.matmul(pw[:, 2, 0:256], xc[:, 4, 0:P], xc[:, 5, :], start=True, stop=True, skip_group_check=True)
                pe.matmul(pw[:, 2, 256:384], xc[:, 4, P:2 * P], xc[:, 5, P:2 * P], start=True, stop=True,
                          skip_group_check=True).then_inc(xt_done, 1)

            def ssd_mix(g):
                wait(pe, x_dt_ready, at(g, 2, 2))
                wait(pe, weights_ready, at(g, 2, 2))
                for h in range(HEADS_PER_GROUP):
                    rows = slice(64 * (h % 2), 64 * (h % 2) + 64)
                    bank, o = 2 + h // 4, 256 * (h // 2 % 2)
                    x = [x_dt[:, t, SSD_HEAD_DIM * h:SSD_HEAD_DIM * (h + 1)] for t in range(2)]
                    pe.matmul(pw[rows, bank, o:o + 256], x[0], weights[:, h, 0:256],
                              start=True, stop=False, skip_group_check=True)
                    mm = pe.matmul(pw[rows, bank, o + P:o + 256], x[1], weights[:, h, 256:384],
                                   start=False, stop=True, skip_group_check=True)
                mm.then_inc(y_done, 1)

            def ssd_norm(g):
                wait(pe, square_summed, at(g, 1, 1))
                pe.matmul(pw[:, 0, 0:256], ones, stat[:], start=True, stop=True,
                          skip_group_check=True).then_inc(norm_summed, 1)

            def ssd(g, first=False, last=False):
                c, b = at(g, C_SSD, 24), at(g, B_SSD, 6)
                for kc in range(4):
                    wide(c, b, kc, 4, X)
                    if kc == 1 and not first:
                        ssd_norm(g - 1)
                for kc in range(4):
                    wide(c + 4, b + 1, kc, 4, X)
                for m in range(2):
                    for kc in range(2):
                        multiply(c + (8 + 2 * m + kc), b + 2, False, (m,), range(8 * kc, 8 * kc + 8),
                                 first=kc == 0, last=kc == 1, **X)
                for kc in range(4):
                    wide(c + 12, b + 3, kc, 4, X)
                ssd_turn_x(g)
                for kc in range(4):
                    wide(c + 16, b + 4, kc, 4, X)
                for kc in range(4):
                    wide(c + 20, b + 5, kc, 4, X)
                    if kc == 0:
                        ssd_mix(g)

            ssd(0, first=True)
            with pe.Fori(1, SSD_GROUPS) as g:
                ssd(g)

            for kc in range(8):
                pe.wait_ge(y_lo_done, kc + 1)
                wide(Count(C_PA), Count(B_PA), kc, 8, Y)
                if kc == 1:
                    ssd_norm(SSD_GROUPS - 1)
            for kc in range(8):
                wide(Count(C_PA + 8), Count(B_PA + 1), kc, 8, Y)
            with pe.Fori(1, 4) as i:
                for n in range(2):
                    for kc in range(8):
                        wide(at(i, C_PA + 8 * n, 16), at(i, B_PA + n, 2), kc, 8, Y)

            for kc in range(4):
                pe.wait_ge(merged_lo_done, 2 * kc + 2)
                wide(Count(C_O), Count(B_O), kc, 4, M)
            for kc in range(4):
                wide(Count(C_O + 4), Count(B_O + 1), kc, 4, M)
            with pe.Fori(1, 4) as i:
                for n in range(2):
                    for kc in range(4):
                        wide(at(i, C_O + 4 * n, 8), at(i, B_O + n, 2), kc, 4, M)

            def layer_norm(n):
                pe.wait_ge(ln_acc_ready, n + 1)
                pe.matmul(pw[:, 0, 0:256], ones, acc[:], start=True, stop=True,
                          skip_group_check=True).then_inc(ln_mean_done, 1)
                for k in range(8):
                    pe.wait_ge(ln_squared, 8 * n + k + 1)
                    mm = pe.matmul(pw[:, 1, :], ones, sq2[:, k % 2, :, :], start=k == 0, stop=k == 7,
                                   skip_group_check=True)
                    mm.then_inc(ln_sq_summed, 1)

            layer_norm(0)

            for kc in range(4):
                pe.wait_ge(x1_lo_done, 4 * kc + 4)
                wide(Count(C_GU), Count(B_GU), kc, 4, X1)
            for kc in range(4):
                wide(Count(C_GU + 4), Count(B_GU + 1), kc, 4, X1)
            with pe.Fori(1, GU_PAIRS) as i:
                for n in range(2):
                    for kc in range(4):
                        wide(at(i, C_GU + 4 * n, 8), at(i, B_GU + n, 2), kc, 4, X1)
            for kc in range(11):
                pe.wait_ge(h_lo_done, 2 * kc + 2)
                wide(Count(C_DN), Count(B_DN), kc, 11, H)
            for n in range(1, 4):
                for kc in range(11):
                    wide(Count(C_DN + 11 * n), Count(B_DN + n), kc, 11, H)
            with pe.Fori(1, 2) as i:
                for n in range(4):
                    for kc in range(11):
                        wide(at(i, C_DN + 11 * n, 44), at(i, B_DN + n, 4), kc, 11, H)
            layer_norm(1)

        @block.scalar
        def _(act):
            A = nc.scalar.activation

            def split(c):
                slot = c.base % RING
                use = Count(16 * (c.base // RING + 1), 16 * c.step // RING, c.i)
                wait(act, raw_landed[slot], use)
                wait(act, chunk_multiplied, c + (1 - RING))
                A(w_hi[:, slot, :], raw[:, slot, :], ACT.Copy).then_inc(hi_split, 1)

            def copy_low(b, c_last, pair=2):
                wait(act, chunk_multiplied, c_last + 1)
                par_ = b.base % 2
                A(low[:, par_, 0:pair, :], ps[:, 2 * par_:2 * par_ + pair, 1, :], ACT.Copy).then_inc(low_copied, 1)

            for c in range(16):
                if c < 4:
                    act.wait_ge(x_landed[c], 16)
                    A(x_hl[:, 4 * c:4 * c + 4, 0, :], x_raw[:, 4 * c:4 * c + 4, :], ACT.Copy).then_inc(x_hi_done, 1)
                split(Count(c))
                if c >= 6 and c % 4 == 2:
                    n = (c - 6) // 4
                    copy_low(Count(n), Count(4 * n + 3))

            def att_exp(j):
                wait(act, shifted, at(j, 1, 1))
                A(sink_d[:], sink_d[:], ACT.Exp)
                A(prob[:], prob[:], ACT.Exp).then_inc(exp_done, 1)

            def att_copy_probs(j):
                wait(act, probs_turned, at(j, 1, 1))
                A(prob_t[:].rearrange("p n t -> p (n t)"), pw[:, 0:3, :].rearrange("p b n -> p (b n)"),
                  ACT.Copy).then_inc(probs_copied, 1)

            def att_hi(j):
                wait(act, att_turned, at(j, 1, 1))
                A(yatt_hl[:, ds(j, 2, 0, 2), 0, :], pw[:, 3, :].rearrange("p (f t) -> p f t", f=2),
                  ACT.Copy).then_inc(yatt_hi_done, 1)

            def attention(j, first=False):
                c, b = at(j, C_ATT, 8), at(j, B_ATT, 2)
                for u in range(8):
                    split(c + u)
                    if u == 2:
                        copy_low(b + (-1), c + (-1))
                    if u == 3 and not first:
                        att_exp(j - 1)
                    if u == 5 and not first:
                        att_copy_probs(j - 1)
                    if u == 6:
                        copy_low(b, c + 3)
                        if first:
                            act.wait_ge(v_turned, 1)
                            A(v_tm[:], pw[:, 0:2, :], ACT.Copy).then_inc(v_ready, 1)
                    if u == 7 and not first:
                        att_hi(j - 1)

            attention(0, first=True)
            with act.Fori(1, KV_HEADS) as j:
                attention(j)

            tail = KV_HEADS - 1

            def gate_sigmoid(i, n, branch, evacuated, done):
                act.wait_ge(block_evacuated, evacuated)
                v = gates[:, ds(i * 2, 2, 2 * n, 2), branch, :]
                A(v, v, ACT.Sigmoid).then_inc(done, 1)

            def pb_block(i, n, extra):
                c, b, prev_last = at(i, C_PB + 4 * n, 8), at(i, B_PB + n, 2), at(i, C_PB + 4 * n - 1, 8)
                for u in range(4):
                    split(c + u)
                    if u == 1:
                        gate_sigmoid(i, n - 1, 1, B_DT, gb_sigmoid)
                    if u == 2:
                        copy_low(b + (-1), prev_last)
                    extra(u)

            split(Count(C_DT))
            split(Count(C_DT + 1))
            split(Count(C_PB))
            copy_low(Count(B_DT - 1), Count(C_DT - 1))
            split(Count(C_PB + 1))
            att_exp(tail)
            split(Count(C_PB + 2))
            copy_low(Count(B_DT), Count(C_PB - 1), pair=1)
            split(Count(C_PB + 3))
            att_copy_probs(tail)
            A(neg_a[:], hd[:, 1:2], ACT.Exp)
            act.wait_ge(dt_neg_abs, 1)
            A(dts[2][:], dts[1][:], ACT.Exp).then_inc(dt_exp, 1)
            split(Count(C_PB + 4))
            split(Count(C_PB + 5))
            att_hi(tail)
            split(Count(C_PB + 6))
            copy_low(Count(B_PB), Count(C_PB + 3))
            gate_sigmoid(0, 0, 1, B_DT, gb_sigmoid)
            split(Count(C_PB + 7))
            with act.Fori(1, 3) as i:
                for n in range(2):
                    pb_block(i, n, lambda u: None)

            def dt_early(u):
                if u == 3:
                    act.wait_ge(dt_turned, 1)
                    A(dt_tm[:].rearrange("p t h -> p (t h)"), pw[:, 0, 0:P], ACT.Copy)
                    A(da_tm[:].rearrange("p t h -> p (t h)"), pw[:, 0, P:2 * P], ACT.Copy).then_inc(dt_copied, 1)

            def dt_late(u):
                if u == 2:
                    act.wait_ge(cum_done, 1)
                    A(dts[0][:], pw[0:64, 2, 0:256], ACT.Copy).then_inc(cum_copied, 1)

            pb_block(3, 0, dt_early)
            pb_block(3, 1, dt_late)
            gate_sigmoid(3, 1, 1, B_DT, gb_sigmoid)

            def conv_silu(g, n):
                wait(act, conv_done, at(g, n + 1, 3))
                v = xc[:, 2 * n:2 * n + 2, :]
                A(v, v, ACT.Silu).then_inc(conv_silu_done, 1)

            def z_silu(g, n):
                wait(act, block_evacuated, at(g, B_SSD + 4 + n, 6))
                v = zc[:, 2 * n:2 * n + 2, :]
                A(v, v, ACT.Silu).then_inc(z_silu_done, 1)

            def ssd_decay(g, half):
                wait(act, seg_ready, at(g, half + 1, 2))
                v = weights[:, 4 * half:4 * half + 4, :]
                A(v, v, ACT.Exp).then_inc(decay_done, 1)

            def ssd_square(g):
                wait(act, gated, at(g, 1, 1))
                A(square[:], xc[:, 0:4, :], ACT.Square).then_inc(squared, 1)

            def ssd_sqrt(g):
                wait(act, var_ready, at(g, 1, 1))
                A(rstd[:], rstd[:], ACT.Sqrt).then_inc(sqrt_done, 1)

            def y_hi_part(n):
                act.wait_ge(y_ready, n + 1)
                act.wait_ge(seg_ready, 2 * SSD_GROUPS)
                o = Y_TILE[n]
                A(y_hi[:, o:o + 4, :], y_plain[:, 4 * n:4 * n + 4, :], ACT.Copy).then_inc(y_hi_done, 1)

            def ssd(g, first=False, last=False):
                c, b = at(g, C_SSD, 24), at(g, B_SSD, 6)
                for u in range(24):
                    split(c + u)
                    if u == 1 and not first:
                        ssd_square(g - 1)
                    if u == 2:
                        copy_low(b + (-1), c + (-1))
                    if u == 5 and not first:
                        ssd_sqrt(g - 1)
                    if u in (18, 19):
                        ssd_decay(g, u - 18)
                    if u in (6, 10):
                        copy_low(b + (u - 6) // 4, c + (u - 3))
                    if u in (9, 12, 15):
                        conv_silu(g, (9, 12, 15).index(u))
                    if u == 14:
                        copy_low(b + 2, c + 11)
                    if u in (18, 22):
                        copy_low(b + 3 + (u - 18) // 4, c + (u - 3))
                    if u in (22, 23):
                        z_silu(g, u - 22)
                    if last and u in (20, 21):
                        y_hi_part(u - 20)

            ssd(0, first=True)
            with act.Fori(1, SSD_GROUPS - 1) as g:
                ssd(g)
            ssd(SSD_GROUPS - 1, last=True)

            def merged_hi(i, n):
                wait(act, merged_ready, at(i, n + 1, 2))
                A(merged_hl[:, ds(i, 4, 2 * n, 2), 0, :], tmp[:], ACT.Copy).then_inc(merged_hi_done, 1)

            last = SSD_GROUPS - 1
            for u in range(8):
                split(Count(C_PA + u))
                if u == 1:
                    ssd_square(last)
                if u == 2:
                    copy_low(Count(B_PA - 1), Count(C_PA - 1))
                if u == 5:
                    ssd_sqrt(last)
                if u >= 2:
                    y_hi_part(u)

            def pa_block(i, n, first=False):
                for u in range(8):
                    split(at(i, C_PA + 8 * n + u, 16))
                    if u == 1:
                        gate_sigmoid(i, n - 1, 0, B_PA, ga_sigmoid)
                    if u == 2:
                        copy_low(at(i, B_PA + n - 1, 2), at(i, C_PA + 8 * n - 1, 16))
                    if u == 4:
                        merged_hi(i, n - 1)

            pa_block(0, 1)
            with act.Fori(1, 4) as i:
                pa_block(i, 0)
                pa_block(i, 1)

            def o_block(i, n, after_pa=False):
                for u in range(4):
                    split(at(i, C_O + 4 * n + u, 8))
                    if u == 1 and after_pa:
                        gate_sigmoid(3, 1, 0, B_PA, ga_sigmoid)
                    if u == 2:
                        copy_low(at(i, B_O + n - 1, 2), at(i, C_O + 4 * n - 1, 8))
                    if u == 3 and after_pa:
                        merged_hi(3, 1)

            o_block(0, 0, after_pa=True)
            o_block(0, 1)
            with act.Fori(1, 4) as i:
                o_block(i, 0)
                o_block(i, 1)

            def layer_norm(n):
                for k in range(8):
                    act.wait_ge(ln_centred, 4 * n + k // 2 + 1)
                    if 8 * n + k >= 2:
                        act.wait_ge(ln_sq_summed, 8 * n + k - 1)
                    A(sq2[:, k % 2, :, :], res[:, 2 * k:2 * k + 2, :], ACT.Square).then_inc(ln_squared, 1)
                act.wait_ge(ln_var_ready, n + 1)
                A(lrstd[:], lstat[:], ACT.Sqrt).then_inc(ln_sqrt_done, 1)
                for k in range(KT):
                    act.wait_ge(ln_scaled, KT * n + k + 1)
                    bias = par[:, LN_COL + KT * (2 * n + 1) + k:LN_COL + KT * (2 * n + 1) + k + 1]
                    if n == 0:
                        A(x1_hl[:, k, 0, :], res[:, k, :], ACT.Identity, bias=bias).then_inc(x1_hi_done, 1)
                    else:
                        A(res[:, k, :], res[:, k, :], ACT.Identity, bias=bias).then_inc(out_ready, 1)

            def h_hi(i):
                wait(act, h_taken, at(i, 1, 1))
                A(h_hl[:, ds(i, 2, 0, 2), 0, :], t2[:], ACT.Copy).then_inc(h_hi_done, 1)

            def gate_up(i, first=False):
                c, b = at(i, C_GU, 8), at(i, B_GU, 2)
                for u in range(8):
                    split(c + u)
                    if u == 2:
                        copy_low(b + (-1), c + (-1))
                    if u == 3:
                        if first:
                            layer_norm(0)
                        else:
                            h_hi(i - 1)
                    if u == 6:
                        copy_low(b, c + 3)
                    if u == 7:
                        wait(act, block_evacuated, b + 1)
                        A(gate_g[:], gate_g[:], ACT.Silu).then_inc(gate_silu, 1)

            gate_up(0, first=True)
            with act.Fori(1, GU_PAIRS) as i:
                gate_up(i)

            def down(i, first=False):
                for n in range(4):
                    c, b = at(i, C_DN + 11 * n, 44), at(i, B_DN + n, 4)
                    for u in range(11):
                        split(c + u)
                        if u == 2:
                            copy_low(b + (-1), c + (-1))
                        if u == 3 and n == 0 and first:
                            h_hi(GU_PAIRS - 1)

            down(0, first=True)
            with act.Fori(1, 2) as i:
                down(i)
            copy_low(Count(B_DN + 7), Count(C_DN + 87))
            layer_norm(1)

        @block.vector
        def _(dve):
            V = nc.vector
            chain = Chain(dve, dve_step)

            def split(c):
                slot = c.base % RING
                wait(dve, hi_split, c + 1)
                V.tensor_tensor(w_lo[:, slot, :], raw[:, slot, :], w_hi[:, slot, :].bitcast(F32),
                                ALU.subtract).then_inc(lo_split, 1)

            def take(b, out, pair=2, rows=P):
                wait(dve, low_copied, b + 1)
                p_ = b.base % 2
                src, lo = ps[0:rows, 2 * p_:2 * p_ + pair, 0, :], low[0:rows, p_, 0:pair, :]
                V.tensor_tensor(out, src, lo, ALU.add).then_inc(block_evacuated, 1)

            def taken(b):
                wait(dve, block_evacuated, b + 1)

            V.memset(kz[:], 0.0).then_inc(dve_step, 1)
            chain.total += 1
            for c in range(16):
                if c < 4:
                    dve.wait_ge(x_hi_done, c + 1)
                    V.tensor_tensor(x_hl[:, 4 * c:4 * c + 4, 1, :], x_raw[:, 4 * c:4 * c + 4, :],
                                    x_hl[:, 4 * c:4 * c + 4, 0, :].bitcast(F32), ALU.subtract).then_inc(x_lo_done, 1)
                split(Count(c))
                if c >= 6 and c % 4 == 2:
                    n = (c - 6) // 4
                    take(Count(n), kv_fm[:, 2 * n:2 * n + 2, :])
            dve.wait_ge(consts_landed, 64)

            def over(v, n):
                return v.unsqueeze(2).to_broadcast([P, 4, n])

            def sink(j):
                return sink_b[:, ds(j, 4, 0, 4)]

            halves = [prob[:, :, 0:P], prob[:, :, P:384]]

            def att_mask(j):
                wait(dve, scores_done, at(j, 1, 1))
                V.scalar_tensor_tensor(halves[0], pw[:, 0, :].rearrange("p (h s) -> p h s", h=4), ATT_SCALE,
                                       band[:, 0:P].unsqueeze(1).to_broadcast([P, 4, P]), ALU.mult, ALU.add)
                for n in range(2):
                    ins = V.scalar_tensor_tensor(prob[:, 2 * n:2 * n + 2, P:384],
                                                 pw[:, 1 + n, :].rearrange("p (h s) -> p h s", h=2), ATT_SCALE,
                                                 band[:, P:384].unsqueeze(1).to_broadcast([P, 2, 256]), ALU.mult, ALU.add)
                chain.link(ins)

            def att_peak(j):
                for t in range(2):
                    ins = V.tensor_reduce(peak[:, t, :], halves[t], AX.X, ALU.max)
                chain.link(ins)
                for t in range(2):
                    ins = V.tensor_tensor(peak[:, t, :], peak[:, t, :], sink(j), ALU.max)
                chain.link(ins)

            def att_shift(j):
                for t in range(2):
                    V.tensor_tensor(halves[t], halves[t], over(peak[:, t, :], P * (t + 1)), ALU.subtract)
                V.tensor_tensor(sink_d[:, 0, :], sink(j), peak[:, 0, :], ALU.subtract)
                V.tensor_tensor(sink_d[:, 1, :], sink(j), peak[:, 1, :], ALU.subtract).then_inc(shifted, 1)

            def att_denominator(j):
                wait(dve, exp_done, at(j, 1, 1))
                for t in range(2):
                    ins = V.tensor_reduce(denom[:, t, :], halves[t], AX.X, ALU.add)
                chain.link(ins)
                chain.link(V.tensor_tensor(denom[:], denom[:], sink_d[:], ALU.add))
                chain.link(V.reciprocal(recip[:], denom[:]))

            def att_scale_out(j):
                wait(dve, att_done, at(j, 1, 1))
                V.tensor_tensor(o_tm[:], pw[:, 3, :].rearrange("p (h d) -> p h d", h=8),
                                recip[:].rearrange("p t h -> p (t h)").unsqueeze(2).to_broadcast([P, 8, ATT_HEAD_DIM]),
                                ALU.mult).then_inc(att_scaled, 1)

            def att_lo(j):
                wait(dve, yatt_hi_done, at(j, 1, 1))
                V.tensor_tensor(yatt_hl[:, ds(j, 2, 0, 2), 1, :], pw[:, 3, :].rearrange("p (f t) -> p f t", f=2),
                                yatt_hl[:, ds(j, 2, 0, 2), 0, :].bitcast(F32), ALU.subtract).then_inc(yatt_lo_done, 1)

            def pick_k(j):
                V.tensor_copy(kz[0:64, 0, :], kd[0:64, ds(j, 1, 0, 1), :].rearrange("p a t -> p (a t)"))
                V.tensor_copy(kz[64:128, 1, :], kd[64:128, ds(j, 1, 0, 1), :].rearrange("p a t -> p (a t)")
                              ).then_inc(k_picked, 1)

            def attention(j, first=False):
                c, b = at(j, C_ATT, 8), at(j, B_ATT, 2)
                for u in range(8):
                    split(c + u)
                    if not first:
                        if u == 0:
                            att_mask(j - 1)
                        if u == 1:
                            att_peak(j - 1)
                        if u == 2:
                            att_shift(j - 1)
                            take(b + (-1), gates[:, ds(j, 2, -2, 2), 1, :])
                        if u == 4:
                            att_denominator(j - 1)
                        if u == 6:
                            att_scale_out(j - 1)
                        if u == 7:
                            att_lo(j - 1)
                    elif u == 2:
                        take(b + (-1), kv_fm[:, 6:8, :])
                    if u == 6:
                        take(b, q_fm[:])
                        if first:
                            dve.wait_ge(k_spread, 64)
                        pick_k(j)
                    if u == 7:
                        if first:
                            dve.wait_ge(v_ready, 1)
                        V.tensor_copy(v_cur[:], v_tm[:, :, ds(j, ATT_HEAD_DIM, 0, ATT_HEAD_DIM)]).then_inc(v_picked, 1)

            attention(0, first=True)
            with dve.Fori(1, KV_HEADS) as j:
                chain.enter(j, 1, 6)
                attention(j)
            chain.leave(KV_HEADS - 1)

            def pb_take(i, n):
                cols = ds(i, 4, 2 * n, 2)
                b = at(i, B_PB + n, 2)
                take(b, tmp[:])
                taken(b)
                wait(dve, gb_sigmoid, at(i, n + 1, 2))
                V.tensor_tensor(gates[:, cols, 1, :], gates[:, cols, 1, :], tmp[:], ALU.mult).then_inc(merged_part, 1)

            def softplus_exponent():
                taken(Count(B_DT))
                chain.link(V.tensor_scalar(dts[0][:], dts[0][:], hd[:, 0:1], None, ALU.add))
                chain.link(V.tensor_scalar(dts[1][:], dts[0][:], -1.0, None, ALU.mult))
                V.tensor_tensor(dts[1][:], dts[1][:], dts[0][:], ALU.min).then_inc(dt_neg_abs, 1)

            e, s, s2, p = dts[2], dts[3], dts[4], dts[1]

            def softplus_argument():
                dve.wait_ge(dt_exp, 1)
                chain.link(V.tensor_scalar(s[:], e[:], 2.0, None, ALU.add))
                chain.link(V.reciprocal(s[:], s[:]))
                chain.link(V.tensor_tensor(s[:], s[:], e[:], ALU.mult))
                chain.link(V.tensor_tensor(s2[:], s[:], s[:], ALU.mult))
                chain.link(V.tensor_scalar(p[:], s2[:], 1.0 / 15, None, ALU.mult))

            def softplus_terms(odds):
                for odd in odds:
                    chain.link(V.scalar_tensor_tensor(p[:], p[:], 1.0 / odd, s2[:], ALU.add, ALU.mult))

            def step_sizes():
                chain.link(V.scalar_tensor_tensor(p[:], p[:], 1.0, s[:], ALU.add, ALU.mult))
                chain.link(V.tensor_scalar(dts[0][:], dts[0][:], 0.0, None, ALU.max))
                chain.link(V.scalar_tensor_tensor(dts[5][:], p[:], 2.0, dts[0][:], ALU.mult, ALU.add))
                V.tensor_scalar(dts[6][:], dts[5][:], neg_a[:], -1.0, ALU.mult, ALU.mult).then_inc(dt_ready, 1)

            tail = KV_HEADS - 1
            split(Count(C_DT))
            att_mask(tail)
            split(Count(C_DT + 1))
            att_peak(tail)
            split(Count(C_PB))
            take(Count(B_DT - 1), gates[:, 14:16, 1, :])
            att_shift(tail)
            split(Count(C_PB + 1))
            split(Count(C_PB + 2))
            att_denominator(tail)
            take(Count(B_DT), dts[0][:].unsqueeze(1), pair=1, rows=SSD_HEADS)
            softplus_exponent()
            split(Count(C_PB + 3))
            split(Count(C_PB + 4))
            att_scale_out(tail)
            split(Count(C_PB + 5))
            att_lo(tail)
            split(Count(C_PB + 6))
            pb_take(0, 0)
            split(Count(C_PB + 7))
            softplus_argument()

            def pb_block(i, n, extra=None):
                for u in range(4):
                    split(at(i, C_PB + 4 * n + u, 8))
                    if u == 2:
                        pb_take(i, n - 1)
                    if extra:
                        extra(u)

            pieces = {0: (13, 11), 1: (9, 7), 3: (5, 3)}
            pb_block(1, 0, lambda u: softplus_terms(pieces[u]) if u in pieces else None)
            pb_block(1, 1, lambda u: step_sizes() if u == 0 else None)
            with dve.Fori(2, 3) as i:
                for n in range(2):
                    pb_block(i, n)

            def neg_cum(u):
                if u == 2:
                    dve.wait_ge(cum_done, 1)
                    chain.link(V.tensor_scalar(ncum[:].rearrange("p t h -> p (t h)"), pw[:, 1, 0:P], -1.0, None, ALU.mult))

            pb_block(3, 0)
            pb_block(3, 1, neg_cum)

            V.memset(conv_in[:], 0.0).then_inc(dve_step, 1)
            chain.total += 1
            chain.wait()

            def pick_cum(g):
                chain.link(V.tensor_copy(ncum_g[:], ncum[:, :, ds(g, HEADS_PER_GROUP, 0, HEADS_PER_GROUP)]))

            def ssd_pick(g):
                wait(dve, y_ready, at(g, 0, 1))
                V.tensor_copy(dt_g[:], dt_tm[:, :, ds(g, HEADS_PER_GROUP, 0, HEADS_PER_GROUP)])
                chain.link(V.tensor_copy(gp[:], par[:, ds(g, GP_WIDTH, 0, GP_WIDTH)]))

            def ssd_seg(g, half):
                wait(dve, c_row_landed, at(g, 16, 16))
                for h in range(4 * half, 4 * half + 4):
                    V.tensor_scalar(weights[:, h, 0:256], c_row[:, h, :], ncum_g[:, 0, h:h + 1], 0.0, ALU.add, ALU.min)
                    ins = V.tensor_scalar(weights[:, h, 256:384], c_row[:, h, P:2 * P], ncum_g[:, 1, h:h + 1], 0.0,
                                          ALU.add, ALU.min)
                ins.then_inc(seg_ready, 1)

            def conv(g, n):
                taken(at(g, B_SSD + n, 6))
                for k in range(CONV_TAPS):
                    for m in range(2):
                        f = 2 * n + m
                        w = gp[:, GP_CONV + 4 * f + k:GP_CONV + 4 * f + k + 1]
                        out, src = xc[:, f, :], conv_in[:, m, k:k + SEQ]
                        if k == 0:
                            ins = V.tensor_scalar(out, src, w, gp[:, GP_BIAS + f:GP_BIAS + f + 1], ALU.mult, ALU.add)
                        else:
                            ins = V.scalar_tensor_tensor(out, src, w, out, ALU.mult, ALU.add)
                    if k < CONV_TAPS - 1:
                        chain.link(ins)
                ins.then_inc(conv_done, 1)

            def ssd_x_dt(g):
                wait(dve, xt_done, at(g, 1, 1))
                for t in range(2):
                    V.tensor_tensor(x_dt[:, t, :].rearrange("p (h d) -> p h d", d=SSD_HEAD_DIM),
                                    pw[:, t, :].rearrange("p (h d) -> p h d", d=SSD_HEAD_DIM),
                                    dt_g[:, t, :].unsqueeze(2).to_broadcast([P, HEADS_PER_GROUP, SSD_HEAD_DIM]),
                                    ALU.mult).then_inc(x_dt_ready, 1)
                chain.link(V.tensor_tensor(cb[:], pw[:, 2, 0:384], causal, ALU.mult))

            def ssd_weights(g, half):
                wait(dve, decay_done, at(g, half + 1, 2))
                v = weights[:, 4 * half:4 * half + 4, :]
                V.tensor_tensor(v, v, cb[:].unsqueeze(1).to_broadcast([P, 4, 384]), ALU.mult).then_inc(weights_ready, 1)

            def ssd_skip(g):
                wait(dve, y_done, at(g, 1, 1))
                for f in range(4):
                    o = 256 * (f % 2)
                    ins = V.scalar_tensor_tensor(xc[:, f, :], xc[:, f, :], gp[:, GP_SKIP + f:GP_SKIP + f + 1],
                                                 pw[:, 2 + f // 2, o:o + 256], ALU.mult, ALU.add)
                chain.link(ins)

            def ssd_gate(g):
                wait(dve, z_silu_done, at(g, 2, 2))
                V.tensor_tensor(xc[:, 0:4, :], xc[:, 0:4, :], zc[:], ALU.mult).then_inc(gated, 1)

            def ssd_square_sum(g):
                wait(dve, squared, at(g, 1, 1))
                V.tensor_reduce(stat[:], square[:].rearrange("p f t -> p t f"), AX.X, ALU.add).then_inc(square_summed, 1)

            def ssd_var(g):
                wait(dve, norm_summed, at(g, 1, 1))
                V.tensor_scalar(rstd[:], pw[:, 0, 0:256], float(SSD_GROUPS) / SSD_INNER, RMS_EPS,
                                ALU.mult, ALU.add).then_inc(var_ready, 1)

            def ssd_rstd(g):
                wait(dve, sqrt_done, at(g, 1, 1))
                chain.link(V.reciprocal(rstd[:], rstd[:]))

            def ssd_out(g):
                wait(dve, gated, at(g, 1, 1))
                for f in range(4):
                    ins = V.scalar_tensor_tensor(y_plain[:, ds(g, 4, f, 1), :].rearrange("p a t -> p (a t)"), xc[:, f, :],
                                                 gp[:, GP_NORM + f:GP_NORM + f + 1], rstd[:], ALU.mult, ALU.mult)
                ins.then_inc(y_ready, 1)

            def y_lo_part(n):
                dve.wait_ge(y_hi_done, n + 1)
                o = Y_TILE[n]
                V.tensor_tensor(y_lo[:, 4 * n:4 * n + 4, :], y_plain[:, 4 * n:4 * n + 4, :],
                                y_hi[:, o:o + 4, :].bitcast(F32), ALU.subtract).then_inc(y_lo_done, 1)

            def ssd(g, first=False, last=False):
                c, b = at(g, C_SSD, 24), at(g, B_SSD, 6)
                conv_cols = conv_in[:, :, CONV_TAPS - 1:CONV_TAPS - 1 + SEQ]
                for u in range(24):
                    split(c + u)
                    if not first:
                        if u == 0:
                            ssd_skip(g - 1)
                        if u == 1:
                            ssd_gate(g - 1)
                        if u == 2:
                            ssd_square_sum(g - 1)
                            take(b + (-1), gates[:, ds(g, 2, -2, 2), 0, :])
                        if u == 5:
                            ssd_var(g - 1)
                        if u == 6:
                            ssd_rstd(g - 1)
                        if u == 7:
                            ssd_out(g - 1)
                    elif u == 2:
                        pb_take(3, 1)
                    if u == 7:
                        ssd_pick(g)
                    if u in (6, 10):
                        take(b + (u - 6) // 4, conv_cols)
                    if u in (8, 11):
                        conv(g, (8, 11).index(u))
                    if u == 14:
                        take(b + 2, conv_cols)
                        conv(g, 2)
                    if u == 16:
                        pick_cum(g)
                    if u in (16, 17):
                        ssd_seg(g, u - 16)
                    if u == 18:
                        take(b + 3, zc[:, 0:2, :])
                        ssd_x_dt(g)
                    if u in (20, 21):
                        ssd_weights(g, u - 20)
                    if u == 22:
                        take(b + 4, zc[:, 2:4, :])
                    if last and u in (22, 23):
                        y_lo_part(u - 22)

            ssd(0, first=True)
            with dve.Fori(1, SSD_GROUPS - 1) as g:
                chain.enter(g, 1, 14)
                ssd(g)
            chain.leave(SSD_GROUPS - 2)
            ssd(SSD_GROUPS - 1, last=True)

            def pa_take(i, n):
                cols = ds(i, 4, 2 * n, 2)
                b = at(i, B_PA + n, 2)
                take(b, tmp[:])
                taken(b)
                wait(dve, ga_sigmoid, at(i, n + 1, 2))
                chain.link(V.tensor_tensor(tmp[:], tmp[:], gates[:, cols, 0, :], ALU.mult))
                V.tensor_tensor(tmp[:], tmp[:], gates[:, cols, 1, :], ALU.add).then_inc(merged_ready, 1)

            def merged_lo(i, n):
                cols = ds(i, 4, 2 * n, 2)
                wait(dve, merged_hi_done, at(i, n + 1, 2))
                V.tensor_tensor(merged_hl[:, cols, 1, :], tmp[:], merged_hl[:, cols, 0, :].bitcast(F32),
                                ALU.subtract).then_inc(merged_lo_done, 1)

            last = SSD_GROUPS - 1
            for u in range(8):
                split(Count(C_PA + u))
                if u == 0:
                    ssd_skip(last)
                if u == 1:
                    ssd_gate(last)
                if u == 2:
                    ssd_square_sum(last)
                    take(Count(B_PA - 1), gates[:, 2 * last:2 * last + 2, 0, :])
                if u == 5:
                    ssd_var(last)
                if u == 6:
                    ssd_rstd(last)
                if u == 7:
                    ssd_out(last)
                if u >= 2:
                    y_lo_part(u)

            def pa_block(i, n):
                for u in range(8):
                    split(at(i, C_PA + 8 * n + u, 16))
                    if u == 2:
                        pa_take(i, n - 1)
                    if u == 5:
                        merged_lo(i, n - 1)

            pa_block(0, 1)
            with dve.Fori(1, 4) as i:
                chain.enter(i, 1, 2)
                pa_block(i, 0)
                pa_block(i, 1)
            chain.leave(3)

            def residual(b, cols, x):
                take(b, t2[:])
                taken(b)
                r = res[:, cols, :]
                chain.link(V.scalar_tensor_tensor(r, x[:, cols, 0, :].bitcast(F32), ALPHA, t2[:], ALU.mult, ALU.add))
                chain.link(V.scalar_tensor_tensor(r, x[:, cols, 1, :].bitcast(F32), ALPHA, r, ALU.mult, ALU.add))

            def add_up(i, step, base, done=None):
                for m in range(2):
                    ins = V.tensor_tensor(acc[:], acc[:], res[:, ds(i, step, base + m, 1), :].rearrange("p a t -> p (a t)"),
                                          ALU.add)
                    if m == 1 and done is not None:
                        ins.then_inc(done, 1)
                    else:
                        chain.link(ins)

            def o_take(i, n, done=None):
                residual(at(i, B_O + n, 2), ds(i, 4, 2 * n, 2), x_hl)
                add_up(i, 4, 2 * n, done)

            def o_block(i, n, after_pa=False):
                for u in range(4):
                    split(at(i, C_O + 4 * n + u, 8))
                    if u == 2:
                        if after_pa:
                            pa_take(3, 1)
                        else:
                            o_take(i, n - 1)
                    if u == 3 and after_pa:
                        merged_lo(3, 1)
                        chain.link(V.memset(acc[:], 0.0))

            o_block(0, 0, after_pa=True)
            o_block(0, 1)
            with dve.Fori(1, 4) as i:
                chain.enter(i, 1, 8)
                o_block(i, 0)
                o_block(i, 1)
            chain.leave(3)

            def layer_norm(n):
                dve.wait_ge(ln_mean_done, n + 1)
                chain.link(V.tensor_scalar(mean[:], pw[:, 0, 0:256], 1.0 / D_MODEL, None, ALU.mult))
                for k in range(4):
                    r = res[:, 4 * k:4 * k + 4, :]
                    V.tensor_tensor(r, r, mean[:].unsqueeze(1).to_broadcast([P, 4, SEQ]), ALU.subtract
                                    ).then_inc(ln_centred, 1)
                dve.wait_ge(ln_sq_summed, 8 * n + 8)
                chain.link(V.tensor_scalar(lstat[:], pw[:, 1, 0:256], 1.0 / D_MODEL, LN_EPS, ALU.mult, ALU.add))
                V.scalar_tensor_tensor(lstat[:], pw[:, 1, 256:512], 1.0 / D_MODEL, lstat[:], ALU.mult, ALU.add
                                       ).then_inc(ln_var_ready, 1)
                dve.wait_ge(ln_sqrt_done, n + 1)
                chain.link(V.reciprocal(lrstd[:], lrstd[:]))
                dve.wait_ge(ln_centred, 4 * n + 4)

                def x1_lo(k):
                    dve.wait_ge(x1_hi_done, k + 1)
                    bias = par[:, LN_COL + KT + k:LN_COL + KT + k + 1]
                    V.scalar_tensor_tensor(x1_hl[:, k, 1, :], res[:, k, :], bias, x1_hl[:, k, 0, :].bitcast(F32),
                                           ALU.add, ALU.subtract).then_inc(x1_lo_done, 1)

                for k in range(KT):
                    gain = par[:, LN_COL + 2 * KT * n + k:LN_COL + 2 * KT * n + k + 1]
                    V.scalar_tensor_tensor(res[:, k, :], res[:, k, :], gain, lrstd[:], ALU.mult, ALU.mult
                                           ).then_inc(ln_scaled, 1)
                    if n == 0 and k >= 2:
                        x1_lo(k - 2)
                if n == 0:
                    x1_lo(KT - 2)
                    x1_lo(KT - 1)

            def up_take(i):
                b = at(i, B_GU + 1, 2)
                take(b, t2[:])
                wait(dve, gate_silu, at(i, 1, 1))
                taken(b)
                V.tensor_tensor(t2[:], t2[:], gate_g[:], ALU.mult).then_inc(h_taken, 1)

            def h_lo(i):
                wait(dve, h_hi_done, at(i, 1, 1))
                cols = ds(i, 2, 0, 2)
                V.tensor_tensor(h_hl[:, cols, 1, :], t2[:], h_hl[:, cols, 0, :].bitcast(F32), ALU.subtract
                                ).then_inc(h_lo_done, 1)

            def gate_up(i, first=False):
                c, b = at(i, C_GU, 8), at(i, B_GU, 2)
                for u in range(8):
                    split(c + u)
                    if u == 2:
                        if first:
                            o_take(3, 1, ln_acc_ready)
                        else:
                            up_take(i - 1)
                    if u == 3 and first:
                        layer_norm(0)
                    if u == 4 and not first:
                        h_lo(i - 1)
                    if u == 6:
                        take(b, gate_g[:])

            gate_up(0, first=True)
            with dve.Fori(1, GU_PAIRS) as i:
                gate_up(i)

            def down_take(i, n, done=None):
                residual(at(i, B_DN + n, 4), ds(i, 8, 2 * n, 2), x1_hl)
                add_up(i, 8, 2 * n, done)

            def down(i, first=False):
                for n in range(4):
                    for u in range(11):
                        split(at(i, C_DN + 11 * n + u, 44))
                        if n == 0 and first:
                            if u == 2:
                                up_take(GU_PAIRS - 1)
                            if u == 4:
                                h_lo(GU_PAIRS - 1)
                                chain.link(V.memset(acc[:], 0.0))
                        elif u == 2:
                            down_take(i, n - 1)

            down(0, first=True)
            with dve.Fori(1, 2) as i:
                chain.enter(i, 1, 16)
                down(i)
            chain.leave(1)
            down_take(1, 3, ln_acc_ready)
            layer_norm(1)


def constants():
    r = np.arange(P)
    cst = np.zeros((P, K_WIDTH), np.float32)
    cst[:, K_ID:K_ID + P] = np.eye(P)
    cst[:, K_ONES:K_ONES + P] = 1.0
    s, l = r[:, None], r[None, :]
    cst[:, K_CUM0:K_CUM0 + P] = -(s > l).astype(np.float32)
    cst[:, K_CUM1:K_CUM1 + P] = s <= l
    cst[:, K_CAUSAL:K_CAUSAL + P] = s <= l
    cst[:, K_CAUSAL + P:K_CAUSAL + 2 * P] = 1.0
    cst[:, K_CAUSAL + 2 * P:K_CAUSAL + 3 * P] = s <= l
    for t in range(2):
        q = (r + P * t)[:, None] // ATT_CHUNK
        k = np.arange(P * (t + 1))[None, :] // ATT_CHUNK
        o = K_BAND + (0 if t == 0 else P)
        cst[:, o:o + P * (t + 1)] = np.where((k == q) | (k == q - 1), 0.0, -1e30)
    return cst


def kernel(**inputs):
    import concourse.bacc as bacc
    from concourse.bass_utils import run_bass_kernel_spmd

    a = {n: np.asarray(v) for n, v in inputs.items()}

    def tiles(v):
        return v.reshape(-1, P).T

    groups = []
    for g in range(SSD_GROUPS):
        feats = [4 * g, 4 * g + 1, 4 * g + 2, 4 * g + 3, KT_Y + g, KT_Y + SSD_GROUPS + g]
        conv = a["conv_w"][0].reshape(CONV_TAPS, -1, P)[:, feats]
        groups.append(conv.transpose(2, 1, 0).reshape(P, -1))
        groups.append(tiles(a["conv_b"][0])[:, feats])
        groups.append(tiles(np.repeat(a["d_skip"][0], SSD_HEAD_DIM))[:, 4 * g:4 * g + 4])
        groups.append(tiles(a["ssd_norm_w"][0])[:, 4 * g:4 * g + 4])
    norms = [tiles(a[n][0]) for n in ("ln1_g", "ln1_b", "ln2_g", "ln2_b")]
    arrays = {
        "x_t": a["x"][0].T,
        "w_in": a["w_in"][0],
        "heads": np.stack([a["dt_bias"][0], a["a_log"][0]], axis=1),
        "sinks": a["sinks"],
        "w_pa": a["w_pa"][0],
        "w_pb": a["w_pb"][0],
        "w_o": a["w_o"][0],
        "w_gu": a["w_gu"][0],
        "w_down": a["w_down"][0],
        "consts": constants(),
        "params": np.concatenate(groups + norms, axis=1),
    }
    nc = bacc.Bacc("TRN2", target_bir_lowering=False, num_devices=1)
    args = []
    for name in arrays:
        arrays[name] = np.ascontiguousarray(arrays[name])
        args.append(nc.dram_tensor(name, arrays[name].shape, mybir.dt.from_np(arrays[name].dtype), kind="ExternalInput").ap())
    out = nc.dram_tensor("out_t", (D_MODEL, SEQ), F32, kind="ExternalOutput").ap()
    hybrid_trunk(nc, *args, out)
    got = run_bass_kernel_spmd(nc, [arrays], core_ids=[0])
    return np.ascontiguousarray(got.results[0]["out_t"].T)[None]
```

```python
from contextlib import ExitStack

import numpy as np
import concourse.bass as bass
from concourse import mybir

F32 = mybir.dt.float32
F32R = mybir.dt.float32r
ACT = mybir.ActivationFunctionType
ALU = mybir.AluOpType
AX = mybir.AxisListType

P = 128
D_MODEL = 2048
SEQ = 256
SSD_INNER = 2 * D_MODEL
SSD_HEADS = 64
SSD_GROUPS = 8
HEADS_PER_GROUP = SSD_HEADS // SSD_GROUPS
SSD_STATE = 128
SSD_HEAD_DIM = 64
CONV_TAPS = 4
CONV_DIM = SSD_INNER + 2 * SSD_GROUPS * SSD_STATE
Q_HEADS = 32
KV_HEADS = 8
ATT_HEAD_DIM = 64
ATT_CHUNK = 64
KV_WIDTH = KV_HEADS * ATT_HEAD_DIM
FFN_HIDDEN = -(-8 * D_MODEL // (3 * 256)) * 256
ALPHA = 2 ** 0.25
ATT_SCALE = ATT_HEAD_DIM ** -0.5
LN_EPS = 1e-5
RMS_EPS = 1e-5

Z_COL = 0
XS_COL = SSD_INNER
B_COL = XS_COL + SSD_INNER
C_COL = B_COL + SSD_GROUPS * SSD_STATE
DT_COL = Z_COL + SSD_INNER + CONV_DIM
Q_COL = DT_COL + SSD_HEADS
K_COL = Q_COL + Q_HEADS * ATT_HEAD_DIM
V_COL = K_COL + KV_WIDTH
GA_COL = V_COL + KV_WIDTH
GB_COL = GA_COL + D_MODEL

RING = 4
CHUNK = 1024
KT = D_MODEL // P
KT_Y = SSD_INNER // P
KT_H = FFN_HIDDEN // P
GU_PAIRS = FFN_HIDDEN // 256

Y_TILE = [12, 16, 0, 4, 8, 20, 24, 28]

C_KV, B_KV = 0, 0
C_ATT, B_ATT = 16, 4
C_DT, B_DT = C_ATT + 8 * KV_HEADS, B_ATT + 2 * KV_HEADS
C_PB, B_PB = C_DT + 2, B_DT + 1
C_SSD, B_SSD = C_PB + 32, B_PB + 8
C_PA, B_PA = C_SSD + 24 * SSD_GROUPS, B_SSD + 6 * SSD_GROUPS
C_O, B_O = C_PA + 64, B_PA + 8
C_GU, B_GU = C_O + 32, B_O + 8
C_DN, B_DN = C_GU + 8 * GU_PAIRS, B_GU + 2 * GU_PAIRS

DVE_BIASES = 2

WARM_START = 9
WARM_LN = (7, 14)

K_ID, K_ONES, K_CUM0, K_CUM1, K_CAUSAL, K_BAND = 0, 128, 256, 384, 512, 896
K_WIDTH = 1280
GP_CONV, GP_BIAS, GP_SKIP, GP_NORM = 0, 24, 30, 34
GP_WIDTH = 38
LN_COL = SSD_GROUPS * GP_WIDTH
PAR_WIDTH = LN_COL + 4 * KT


class Count:

    def __init__(self, base, step=0, i=None):
        self.base, self.step, self.i = base, step, i

    def __add__(self, n):
        return Count(self.base + n, self.step, self.i)

    def value(self):
        return self.base if self.i is None else self.i * self.step + self.base


def at(i, base, step):
    return Count(base + step * i) if isinstance(i, int) else Count(base, step, i)


def wait(eng, sem, count):
    count = count if isinstance(count, Count) else Count(count)
    if count.i is None and count.base <= 0:
        return
    eng.wait_ge(sem, count.value())


class Chain:

    def __init__(self, eng, sem):
        self.eng, self.sem, self.total, self.loop = eng, sem, 0, None

    def mark(self, ins):
        ins.then_inc(self.sem, 1)
        self.total += 1

    def wait(self):
        if self.loop is None:
            self.eng.wait_ge(self.sem, self.total)
        else:
            i, first, per, entry = self.loop
            self.eng.wait_ge(self.sem, i * per + (self.total - first * per))

    def link(self, ins):
        self.mark(ins)
        self.wait()

    def enter(self, i, first, per):
        self.loop = (i, first, per, self.total)

    def leave(self, times):
        i, first, per, entry = self.loop
        assert self.total - entry == per, self.total - entry
        self.total = entry + per * times
        self.loop = None


def ds(i, step, base, size):
    if isinstance(i, int):
        return slice(i * step + base, i * step + base + size)
    return bass.ds(i * step + base, size)


def hybrid_trunk(nc, x_t, w_in, heads, sinks, w_pa, w_pb, w_o, w_gu, w_down, consts, params, out_t):
    with ExitStack() as ctx:
        def sem(name):
            return ctx.enter_context(nc.semaphore(name))

        KB = 1024
        arena = (nc.sbuf_base + 63) // 64 * 64
        place = [arena]

        def put(name, shape, dtype, offset=None):
            size = 4
            for n in shape[1:]:
                size *= n
            if offset is None:
                offset = place[0]
                place[0] += (size + 31) // 32 * 32
            assert offset + size <= nc.sbuf_usable_end, (name, offset + size)
            return nc.alloc_sbuf_tensor_at(name, shape, dtype, offset=offset)

        raw = put("raw", [P, RING, CHUNK], F32)
        w_hi = put("w_hi", [P, RING, CHUNK], F32R)
        w_lo = put("w_lo", [P, RING, CHUNK], F32R)
        low = put("low", [P, 2, 2, SEQ], F32)
        cst = put("cst", [P, K_WIDTH], F32)
        par = put("par", [P, PAR_WIDTH], F32)
        sink_b = put("sink_b", [P, Q_HEADS], F32)
        hd = put("hd", [SSD_HEADS, 2], F32)
        ln_eps = put("ln_eps", [P, 1], F32)
        x_at = place[0]
        x_hl = put("x_hl", [P, KT, 2, SEQ], F32R)
        x1_hl = put("x1_hl", [P, KT, 2, SEQ], F32R, x_at)
        g_at = place[0]
        gates = put("gates", [P, KT, 2, SEQ], F32)
        merged_hl = put("merged_hl", [P, KT, 2, SEQ], F32R, g_at)
        w_at = place[0]
        h_hl = put("h_hl", [P, KT_H, 2, SEQ], F32R, g_at)

        yatt_hl = put("yatt_hl", [P, KT, 2, SEQ], F32R, w_at)
        place[0] = w_at + 32 * KB
        x_raw = put("x_raw", [P, KT, SEQ], F32)
        kd = put("kd", [P, KV_HEADS, SEQ], F32)
        kz = put("kz", [P, 2, SEQ], F32)
        v_tm = put("v_tm", [P, 2, KV_WIDTH], F32)
        v_cur = put("v_cur", [P, 2, ATT_HEAD_DIM], F32)
        q_fm = put("q_fm", [P, 2, SEQ], F32)
        prob = put("prob", [P, 4, 384], F32, place[0])
        kv_fm = put("kv_fm", [P, 8, SEQ], F32, w_at)
        place[0] += 6 * KB
        prob_t = put("prob_t", [P, 12, P], F32)
        o_tm = put("o_tm", [P, 8, ATT_HEAD_DIM], F32)
        peak = put("peak", [P, 2, 4], F32)
        sink_d = put("sink_d", [P, 2, 4], F32)
        denom = put("denom", [P, 2, 4], F32)
        recip = put("recip", [P, 2, 4], F32)

        y_plain = put("y_plain", [P, KT_Y, SEQ], F32, w_at)
        y_lo = put("y_lo", [P, KT_Y, SEQ], F32R, w_at)
        y_hi = put("y_hi", [P, KT_Y, SEQ], F32R, w_at + 32 * KB)
        place[0] = w_at + 32 * KB
        weights = put("weights", [P, HEADS_PER_GROUP, 384], F32)
        c_row = put("c_row", [P, HEADS_PER_GROUP, SEQ], F32)
        x_dt = put("x_dt", [P, 2, HEADS_PER_GROUP * SSD_HEAD_DIM], F32)
        square = put("square", [P, 4, SEQ], F32)
        conv_in = put("conv_in", [P, 2, SEQ + 4], F32)
        cb = put("cb", [P, 384], F32)
        place[0] = max(place[0], w_at + 64 * KB)
        xc = put("xc", [P, 6, SEQ], F32)
        zc = put("zc", [P, 4, SEQ], F32)
        stat = put("stat", [P, SEQ], F32)
        rstd = put("rstd", [P, SEQ], F32)
        tmp = put("tmp", [P, 2, SEQ], F32)
        dt_tm = put("dt_tm", [P, 2, SSD_HEADS], F32)
        ncum = put("ncum", [P, 2, SSD_HEADS], F32)
        ncum_g = put("ncum_g", [P, 2, HEADS_PER_GROUP], F32)
        dt_g = put("dt_g", [P, 2, HEADS_PER_GROUP], F32)
        gp = put("gp", [P, GP_WIDTH], F32)
        dts = [put(f"dts{n}", [SSD_HEADS, SEQ], F32, w_at + 32 * KB + n * KB) for n in range(7)]
        da_tm = put("da_tm", [P, 2, SSD_HEADS], F32, w_at + 39 * KB)
        neg_a = put("neg_a", [SSD_HEADS, 1], F32, w_at + 40 * KB)

        f_at = g_at + KT_H * 2 * KB
        assert f_at >= w_at + 56 * KB - 64
        place[0] = f_at
        res = put("res", [P, KT, SEQ], F32)
        acc = put("acc", [P, 2, SEQ], F32)
        t2 = put("t2", [P, 2, SEQ], F32)
        sq_at = place[0]
        sq4 = put("sq4", [P, 4, SEQ], F32)
        gate_g = put("gate_g", [P, 2, SEQ], F32, sq_at)
        delta = put("delta", [P, SEQ], F32, sq_at)
        lstat = put("lstat", [P, SEQ], F32, sq_at + KB)
        sq2 = put("sq2", [P, 2, SEQ], F32, sq_at + 2 * KB)
        term_at = place[0]
        x_term = put("x_term", [P, 2, SEQ], F32)
        delta_sq = put("delta_sq", [P, SEQ], F32, term_at)
        lrstd = put("lrstd", [P, SEQ], F32, term_at + KB)
        shift = put("shift", [P, SEQ], F32)

        ident = cst[:, K_ID:K_ID + P]
        ones = cst[:, K_ONES:K_ONES + P]
        cum = [cst[:, K_CUM0:K_CUM0 + P], cst[:, K_CUM1:K_CUM1 + P]]
        causal = cst[:, K_CAUSAL:K_CAUSAL + 384]
        band = cst[:, K_BAND:K_BAND + 384]

        ps = ctx.enter_context(nc.psum_tensor("ps", [P, 4, 2, SEQ], F32))
        pw = ctx.enter_context(nc.psum_tensor("pw", [P, 4, 512], F32))

        c_rows = nc.dram_tensor("c_rows", (SSD_GROUPS, HEADS_PER_GROUP * SEQ), F32, kind="Internal").ap()

        x_landed = [sem(f"x_landed{n}") for n in range(4)]
        consts_landed = sem("consts_landed")
        raw_landed = [sem(f"raw_landed{n}") for n in range(RING)]
        hi_split = sem("hi_split")
        lo_split = sem("lo_split")
        chunk_multiplied = sem("chunk_multiplied")
        low_copied = sem("low_copied")
        block_evacuated = sem("block_evacuated")
        x_hi_done, x_lo_done = sem("x_hi_done"), sem("x_lo_done")
        k_spread, v_turned, v_ready = sem("k_spread"), sem("v_turned"), sem("v_ready")
        k_picked, v_picked = sem("k_picked"), sem("v_picked")
        scores_done, shifted, exp_done = sem("scores_done"), sem("shifted"), sem("exp_done")
        probs_turned, probs_copied = sem("probs_turned"), sem("probs_copied")
        att_done, att_scaled, att_turned = sem("att_done"), sem("att_scaled"), sem("att_turned")
        yatt_hi_done, yatt_lo_done = sem("yatt_hi_done"), sem("yatt_lo_done")
        gb_sigmoid, ga_sigmoid = sem("gb_sigmoid"), sem("ga_sigmoid")
        dt_neg_abs, dt_exp, dt_ready, dt_turned = sem("dt_neg_abs"), sem("dt_exp"), sem("dt_ready"), sem("dt_turned")
        dt_copied, cum_done, cum_copied, cum_stored = sem("dt_copied"), sem("cum_done"), sem("cum_copied"), sem("cum_stored")
        c_row_landed = sem("c_row_landed")
        seg_ready, decay_done = sem("seg_ready"), sem("decay_done")
        conv_done, conv_silu_done, z_silu_done = sem("conv_done"), sem("conv_silu_done"), sem("z_silu_done")
        xt_done, x_dt_ready = sem("xt_done"), sem("x_dt_ready")
        weights_ready, y_done = sem("weights_ready"), sem("y_done")
        gated, squared, square_summed = sem("gated"), sem("squared"), sem("square_summed")
        norm_summed, var_ready, sqrt_done, y_ready = sem("norm_summed"), sem("var_ready"), sem("sqrt_done"), sem("y_ready")
        y_hi_done, y_lo_done = sem("y_hi_done"), sem("y_lo_done")
        merged_ready, merged_hi_done, merged_lo_done = sem("merged_ready"), sem("merged_hi_done"), sem("merged_lo_done")
        ln_acc_ready, ln_summed, ln_shifted = sem("ln_acc_ready"), sem("ln_summed"), sem("ln_shifted")
        ln_squared, ln_sq_ready, ln_sq_summed = sem("ln_squared"), sem("ln_sq_ready"), sem("ln_sq_summed")
        ln_var_ready = sem("ln_var_ready")
        ln_sqrt_done, ln_scaled = sem("ln_sqrt_done"), sem("ln_scaled")
        x1_hi_done, x1_lo_done = sem("x1_hi_done"), sem("x1_lo_done")
        gate_silu, h_taken, h_hi_done, h_lo_done = (
            sem("gate_silu"), sem("h_taken"), sem("h_hi_done"), sem("h_lo_done"))
        out_ready_dve = sem("out_ready_dve")
        out_ready, out_stored = sem("out_ready"), sem("out_stored")
        dve_step = sem("dve_step")

        block = ctx.enter_context(nc.Block())

        @block.sync
        def _(sp):
            def load(c, src):
                wait(sp, lo_split, c + (1 - RING))
                slot = c.base % RING
                n = src.shape[2]
                sp.dma_start(raw[:, slot, :].rearrange("p (k n) -> p k n", n=n), src).then_inc(raw_landed[slot], 16)

            def wide(w, kc, cols):
                return w[kc * 512:(kc + 1) * 512, cols].rearrange("(k p) n -> p k n", p=P)

            def tall(w, kc, cols):
                return w[kc * 1024:(kc + 1) * 1024, cols].rearrange("(k p) n -> p k n", p=P)

            def load_block(c, w, cols, n):
                for kc in range(n):
                    load(c + kc, wide(w, kc, cols))

            for n in range(4):
                for kc in range(4):
                    if n == 0:
                        sp.dma_start(x_raw[:, 4 * kc:4 * kc + 4, :], x_t[512 * kc:512 * kc + 512].rearrange(
                            "(k p) t -> p k t", p=P)).then_inc(x_landed[kc], 16)
                    load(Count(C_KV + 4 * n + kc), wide(w_in, kc, slice(K_COL + 256 * n, K_COL + 256 * (n + 1))))

            with sp.Fori(0, KV_HEADS) as j:
                c = at(j, C_ATT, 8)
                load_block(c, w_in, ds(j, 256, Q_COL, 256), 4)
                load_block(c + 4, w_in, ds(j, 256, GB_COL, 256), 4)

            for kc in range(2):
                load(Count(C_DT + kc), tall(w_in, kc, slice(DT_COL, DT_COL + P)))

            with sp.Fori(0, 4) as i:
                for b in range(2):
                    load_block(at(i, C_PB + 4 * b, 8), w_pb, ds(i, 512, 256 * b, 256), 4)

            with sp.Fori(0, SSD_GROUPS) as g:
                c = at(g, C_SSD, 24)
                for b in range(2):
                    load_block(c + 4 * b, w_in, ds(g, 512, XS_COL + 256 * b, 256), 4)
                for kc in range(2):
                    load(c + (8 + kc), tall(w_in, kc, ds(g, P, B_COL, P)))
                for kc in range(2):
                    load(c + (10 + kc), tall(w_in, kc, ds(g, P, C_COL, P)))
                for b in range(2):
                    load_block(c + (12 + 4 * b), w_in, bass.ds((g * 256) * 2 + (Z_COL + 256 * b), 256), 4)
                load_block(c + 20, w_in, ds(g, 256, GA_COL, 256), 4)

            with sp.Fori(0, 4) as i:
                for b in range(2):
                    load_block(at(i, C_PA + 8 * b, 16), w_pa, ds(i, 512, 256 * b, 256), 8)

            with sp.Fori(0, 4) as i:
                for b in range(2):
                    load_block(at(i, C_O + 4 * b, 8), w_o, ds(i, 512, 256 * b, 256), 4)

            with sp.Fori(0, GU_PAIRS) as i:
                load_block(at(i, C_GU, 8), w_gu, ds(i, 256, 0, 256), 4)
                load_block(at(i, C_GU + 4, 8), w_gu, ds(i, 256, FFN_HIDDEN, 256), 4)

            with sp.Fori(0, 2) as i:
                for b in range(4):
                    load_block(at(i, C_DN + 11 * b, 44), w_down, ds(i, 1024, 256 * b, 256), 11)

            out_v = out_t.rearrange("(k p) t -> p k t", p=P)
            for n in range(4):
                sp.wait_ge(out_ready, min(4 * (n + 1), KT - DVE_BIASES))
                if n == 3:
                    sp.wait_ge(out_ready_dve, DVE_BIASES)
                sp.dma_start(out_v[:, 4 * n:4 * n + 4, :], res[:, 4 * n:4 * n + 4, :]).then_inc(out_stored, 16)
            sp.wait_ge(out_stored, 64)

        @block.gpsimd
        def _(pool):
            for n in range(4):
                pool.wait_ge(x_landed[n], 16)
            pool.dma_start(cst[:], consts).then_inc(consts_landed, 16)
            pool.dma_start(par[:], params).then_inc(consts_landed, 16)
            pool.dma_start(sink_b[:], sinks.to_broadcast([P, Q_HEADS])).then_inc(consts_landed, 16)
            pool.dma_start(hd[:], heads).then_inc(consts_landed, 16)
            pool.wait_ge(block_evacuated, B_KV + 2)
            for half in range(2):
                for odd in range(2):
                    dst = kd[64 * half:64 * half + 64].rearrange("p (a b) t -> p b a t", b=2)[:, odd]
                    pool.dma_start(dst, kv_fm[64 * odd:64 * odd + 64, 0:4, :]).then_inc(k_spread, 16)
            pool.wait_ge(cum_copied, 1)
            pool.dma_start(c_rows.rearrange("g (h t) -> (g h) t", h=HEADS_PER_GROUP), dts[0][:]).then_inc(cum_stored, 16)
            pool.wait_ge(cum_stored, 16)

            def spread_rows(g):
                pool.dma_start(c_row[:].rearrange("p h t -> p (h t)"),
                               c_rows[ds(g, 1, 0, 1), :].to_broadcast([P, HEADS_PER_GROUP * SEQ])
                               ).then_inc(c_row_landed, 16)

            spread_rows(0)
            with pool.Fori(1, SSD_GROUPS) as g:
                wait(pool, seg_ready, at(g, 0, 2))
                spread_rows(g)

        @block.tensor
        def _(pe):
            def multiply(c, b, wide, pair, kts, rhs_hi, rhs_lo, rhs_hl, first, last):
                wait(pe, lo_split, c + 1)
                if first:
                    wait(pe, block_evacuated, b + (-1))
                slot = c.base % RING
                mm = None
                for m in pair:
                    bank = 2 * (b.base % 2) + m
                    for n, kt in enumerate(kts):
                        o = n * 256 + m * P if wide else n * P
                        start = first and n == 0
                        if rhs_hl is not None:
                            pe.matmul(ps[:, bank, :, :], w_hi[:, slot, o:o + P], rhs_hl(kt),
                                      start=start, stop=False, skip_group_check=True)
                        else:
                            pe.matmul(ps[:, bank, 0, :], w_hi[:, slot, o:o + P], rhs_hi(kt),
                                      start=start, stop=False, skip_group_check=True)
                            pe.matmul(ps[:, bank, 1, :], w_hi[:, slot, o:o + P], rhs_lo(kt),
                                      start=False, stop=False, skip_group_check=True)
                        mm = pe.matmul(ps[:, bank, 1, :], w_lo[:, slot, o:o + P], rhs_hi(kt),
                                       start=False, stop=last and n == len(kts) - 1, skip_group_check=True)
                mm.then_inc(chunk_multiplied, 1)

            def hl(buf):
                return dict(rhs_hi=lambda kt: buf[:, kt, 0, :], rhs_lo=None, rhs_hl=lambda kt: buf[:, kt, :, :])

            def keep_warm(times, operand):
                for n in range(times):
                    pe.matmul(pw[:, 3, 0:256], operand[:, 0:P], operand[:, 0:256], start=True, stop=True,
                              skip_group_check=True)

            X, YA, M, X1, H = hl(x_hl), hl(yatt_hl), hl(merged_hl), hl(x1_hl), hl(h_hl)
            Y = dict(rhs_hi=lambda kt: y_hi[:, Y_TILE[kt // 4] + kt % 4, :], rhs_lo=lambda kt: y_lo[:, kt, :], rhs_hl=None)

            def wide(c, b, kc, n, src):
                multiply(c + kc, b, True, (0, 1), range(4 * kc, 4 * kc + 4), first=kc == 0, last=kc == n - 1, **src)

            def tall(c, b, kc, m, src):
                multiply(c + kc, b, False, (m,), range(8 * kc, 8 * kc + 8), first=kc == 0, last=kc == 1, **src)

            def turn(out, in_):
                return pe.transpose(out, in_, ident)

            pe.wait_ge(dve_step, 1)
            keep_warm(WARM_START, kz[:, 0, :])
            for n in range(4):
                for kc in range(4):
                    if n == 0:
                        pe.wait_ge(x_lo_done, kc + 1)
                    wide(Count(C_KV + 4 * n), Count(B_KV + n), kc, 4, X)

            def att_scores(j):
                wait(pe, block_evacuated, at(j, B_ATT + 1, 2))
                wait(pe, k_picked, at(j, 1, 1))
                for h in range(4):
                    kk = kz[:, h % 2, :]
                    pe.matmul(pw[:, 0, P * h:P * h + P], q_fm[:, h // 2, 0:P], kk[:, 0:P],
                              start=True, stop=True, skip_group_check=True)
                    mm = pe.matmul(pw[:, 1 + h // 2, 256 * (h % 2):256 * (h % 2) + 256], q_fm[:, h // 2, P:2 * P], kk,
                                   start=True, stop=True, skip_group_check=True)
                mm.then_inc(scores_done, 1)

            def att_turn_probs(j):
                wait(pe, exp_done, at(j, 1, 1))
                for n in range(12):
                    mm = turn(pw[:, n // 4, P * (n % 4):P * (n % 4) + P], prob[:, n // 3, P * (n % 3):P * (n % 3) + P])
                mm.then_inc(probs_turned, 1)

            def att_values(j):
                wait(pe, probs_copied, at(j, 1, 1))
                wait(pe, v_picked, at(j, 1, 1))
                for h in range(4):
                    o = ATT_HEAD_DIM * h
                    pe.matmul(pw[:, 3, o:o + 64], prob_t[:, 3 * h, :], v_cur[:, 0, :],
                              start=True, stop=True, skip_group_check=True)
                    pe.matmul(pw[:, 3, 256 + o:256 + o + 64], prob_t[:, 3 * h + 1, :], v_cur[:, 0, :],
                              start=True, stop=False, skip_group_check=True)
                    mm = pe.matmul(pw[:, 3, 256 + o:256 + o + 64], prob_t[:, 3 * h + 2, :], v_cur[:, 1, :],
                                   start=False, stop=True, skip_group_check=True)
                mm.then_inc(att_done, 1)

            def att_turn_out(j):
                wait(pe, att_scaled, at(j, 1, 1))
                for f in range(2):
                    for t in range(2):
                        mm = turn(pw[:, 3, 256 * f + P * t:256 * f + P * t + P],
                                  o_tm[:, 4 * t + 2 * f:4 * t + 2 * f + 2, :].rearrange("p h d -> p (h d)"))
                mm.then_inc(att_turned, 1)

            pe.wait_ge(consts_landed, 64)

            def attention(j, first=False):
                c, b = at(j, C_ATT, 8), at(j, B_ATT, 2)
                before = j - 1
                for kc in range(3):
                    wide(c, b, kc, 4, X)
                if not first:
                    att_turn_probs(before)
                wide(c, b, 3, 4, X)
                if first:
                    pe.wait_ge(block_evacuated, B_KV + 4)
                    for f in range(4):
                        for t in range(2):
                            mm = turn(pw[:, t, P * f:P * f + P], kv_fm[:, 4 + f, P * t:P * t + P])
                    mm.then_inc(v_turned, 1)
                else:
                    att_values(before)
                wide(c + 4, b + 1, 0, 4, X)
                if not first:
                    att_turn_out(before)
                wide(c + 4, b + 1, 1, 4, X)
                if first:
                    pe.wait_ge(v_ready, 1)
                att_scores(j)
                for kc in range(2, 4):
                    wide(c + 4, b + 1, kc, 4, X)

            attention(0, first=True)
            with pe.Fori(1, KV_HEADS) as j:
                attention(j)

            for kc in range(2):
                tall(Count(C_DT), Count(B_DT), kc, 0, X)
            tail = KV_HEADS - 1
            c, b = Count(C_PB), Count(B_PB)
            pe.wait_ge(yatt_lo_done, tail)
            wide(c, b, 0, 4, YA)
            att_turn_probs(tail)
            wide(c, b, 1, 4, YA)
            att_values(tail)
            wide(c, b, 2, 4, YA)
            att_turn_out(tail)
            pe.wait_ge(yatt_lo_done, KV_HEADS)
            wide(c, b, 3, 4, YA)
            for kc in range(4):
                wide(c + 4, b + 1, kc, 4, YA)
            with pe.Fori(1, 3) as i:
                for n in range(2):
                    for kc in range(4):
                        wide(at(i, C_PB + 4 * n, 8), at(i, B_PB + n, 2), kc, 4, YA)
            c, b = Count(C_PB + 24), Count(B_PB + 6)
            wide(c, b, 0, 4, YA)
            pe.wait_ge(dt_ready, 1)
            for t in range(2):
                pe.transpose(pw[:, 0, 64 * t:64 * t + 64], dts[5][:, P * t:P * t + P], cst[0:64, K_ID:K_ID + 64])
                mm = pe.transpose(pw[:, 0, P + 64 * t:P + 64 * t + 64], dts[6][:, P * t:P * t + P], cst[0:64, K_ID:K_ID + 64])
            mm.then_inc(dt_turned, 1)
            for kc in range(1, 4):
                wide(c, b, kc, 4, YA)
            pe.wait_ge(dt_copied, 1)
            for t in range(2):
                pe.matmul(pw[:, 1, 64 * t:64 * t + 64], cum[t], da_tm[:, t, :], start=True, stop=True,
                          skip_group_check=True)
                mm = pe.matmul(pw[0:64, 2, P * t:P * t + P], da_tm[:, t, :], cum[t], start=True, stop=True,
                               skip_group_check=True)
            mm.then_inc(cum_done, 1)
            for kc in range(4):
                wide(c + 4, b + 1, kc, 4, YA)

            def ssd_turn_x(g):
                wait(pe, conv_silu_done, at(g, 3, 3))
                for f in range(4):
                    for t in range(2):
                        turn(pw[:, t, P * f:P * f + P], xc[:, f, P * t:P * t + P])
                pe.matmul(pw[:, 2, 0:256], xc[:, 4, 0:P], xc[:, 5, :], start=True, stop=True, skip_group_check=True)
                pe.matmul(pw[:, 2, 256:384], xc[:, 4, P:2 * P], xc[:, 5, P:2 * P], start=True, stop=True,
                          skip_group_check=True).then_inc(xt_done, 1)

            def ssd_mix(g):
                wait(pe, x_dt_ready, at(g, 2, 2))
                wait(pe, weights_ready, at(g, 2, 2))
                for h in range(HEADS_PER_GROUP):
                    rows = slice(64 * (h % 2), 64 * (h % 2) + 64)
                    bank, o = 2 + h // 4, 256 * (h // 2 % 2)
                    x = [x_dt[:, t, SSD_HEAD_DIM * h:SSD_HEAD_DIM * (h + 1)] for t in range(2)]
                    pe.matmul(pw[rows, bank, o:o + 256], x[0], weights[:, h, 0:256],
                              start=True, stop=False, skip_group_check=True)
                    mm = pe.matmul(pw[rows, bank, o + P:o + 256], x[1], weights[:, h, 256:384],
                                   start=False, stop=True, skip_group_check=True)
                mm.then_inc(y_done, 1)

            def ssd_norm(g):
                wait(pe, square_summed, at(g, 1, 1))
                pe.matmul(pw[:, 0, 0:256], ones, stat[:], start=True, stop=True,
                          skip_group_check=True).then_inc(norm_summed, 1)

            def ssd(g, first=False, last=False):
                c, b = at(g, C_SSD, 24), at(g, B_SSD, 6)
                for kc in range(4):
                    wide(c, b, kc, 4, X)
                    if kc == 1 and not first:
                        ssd_norm(g - 1)
                for kc in range(4):
                    wide(c + 4, b + 1, kc, 4, X)
                for m in range(2):
                    for kc in range(2):
                        multiply(c + (8 + 2 * m + kc), b + 2, False, (m,), range(8 * kc, 8 * kc + 8),
                                 first=kc == 0, last=kc == 1, **X)
                for kc in range(4):
                    wide(c + 12, b + 3, kc, 4, X)
                ssd_turn_x(g)
                for kc in range(4):
                    wide(c + 16, b + 4, kc, 4, X)
                for kc in range(4):
                    wide(c + 20, b + 5, kc, 4, X)
                    if kc == 0:
                        ssd_mix(g)

            ssd(0, first=True)
            with pe.Fori(1, SSD_GROUPS) as g:
                ssd(g)

            for kc in range(8):
                pe.wait_ge(y_lo_done, kc + 1)
                wide(Count(C_PA), Count(B_PA), kc, 8, Y)
                if kc == 1:
                    ssd_norm(SSD_GROUPS - 1)
            for kc in range(8):
                wide(Count(C_PA + 8), Count(B_PA + 1), kc, 8, Y)
            with pe.Fori(1, 4) as i:
                for n in range(2):
                    for kc in range(8):
                        wide(at(i, C_PA + 8 * n, 16), at(i, B_PA + n, 2), kc, 8, Y)

            for kc in range(4):
                pe.wait_ge(merged_lo_done, 2 * kc + 2)
                wide(Count(C_O), Count(B_O), kc, 4, M)
            for kc in range(4):
                wide(Count(C_O + 4), Count(B_O + 1), kc, 4, M)

            def ln_sum(count):
                pe.wait_ge(ln_acc_ready, count)
                pe.matmul(pw[:, 0, 0:256], ones, acc[:, 0, :], start=True, stop=True,
                          skip_group_check=True).then_inc(ln_summed, 1)

            def layer_norm(n):
                keep_warm(WARM_LN[0], cst)
                ln_sum(2 * n + 2)
                pe.wait_ge(ln_sq_ready, n + 1)
                pe.matmul(pw[:, 1, 0:256], ones, acc[:, 1, :], start=True, stop=True,
                          skip_group_check=True).then_inc(ln_sq_summed, 1)

            for n in range(2):
                for kc in range(4):
                    wide(Count(C_O + 8 + 4 * n), Count(B_O + 2 + n), kc, 4, M)
                    if n == 0 and kc == 1:
                        ln_sum(1)
            with pe.Fori(2, 4) as i:
                for n in range(2):
                    for kc in range(4):
                        wide(at(i, C_O + 4 * n, 8), at(i, B_O + n, 2), kc, 4, M)
            layer_norm(0)
            keep_warm(WARM_LN[1], cst)

            for kc in range(4):
                pe.wait_ge(x1_lo_done, 4 * kc + 4)
                wide(Count(C_GU), Count(B_GU), kc, 4, X1)
            for kc in range(4):
                wide(Count(C_GU + 4), Count(B_GU + 1), kc, 4, X1)
            with pe.Fori(1, GU_PAIRS) as i:
                for n in range(2):
                    for kc in range(4):
                        wide(at(i, C_GU + 4 * n, 8), at(i, B_GU + n, 2), kc, 4, X1)
            for kc in range(11):
                pe.wait_ge(h_lo_done, 2 * kc + 2)
                wide(Count(C_DN), Count(B_DN), kc, 11, H)
            for n in range(1, 4):
                for kc in range(11):
                    wide(Count(C_DN + 11 * n), Count(B_DN + n), kc, 11, H)
                    if n == 2 and kc == 1:
                        ln_sum(3)
            with pe.Fori(1, 2) as i:
                for n in range(4):
                    for kc in range(11):
                        wide(at(i, C_DN + 11 * n, 44), at(i, B_DN + n, 4), kc, 11, H)
            layer_norm(1)

        @block.scalar
        def _(act):
            A = nc.scalar.activation

            def split(c):
                slot = c.base % RING
                use = Count(16 * (c.base // RING + 1), 16 * c.step // RING, c.i)
                wait(act, raw_landed[slot], use)
                wait(act, chunk_multiplied, c + (1 - RING))
                A(w_hi[:, slot, :], raw[:, slot, :], ACT.Copy).then_inc(hi_split, 1)

            def copy_low(b, c_last, pair=2):
                wait(act, chunk_multiplied, c_last + 1)
                par_ = b.base % 2
                A(low[:, par_, 0:pair, :], ps[:, 2 * par_:2 * par_ + pair, 1, :], ACT.Copy).then_inc(low_copied, 1)

            for c in range(16):
                if c < 4:
                    act.wait_ge(x_landed[c], 16)
                    A(x_hl[:, 4 * c:4 * c + 4, 0, :], x_raw[:, 4 * c:4 * c + 4, :], ACT.Copy).then_inc(x_hi_done, 1)
                split(Count(c))
                if c >= 6 and c % 4 == 2:
                    n = (c - 6) // 4
                    copy_low(Count(n), Count(4 * n + 3))

            def att_exp(j):
                wait(act, shifted, at(j, 1, 1))
                A(sink_d[:], sink_d[:], ACT.Exp)
                A(prob[:], prob[:], ACT.Exp).then_inc(exp_done, 1)

            def att_copy_probs(j):
                wait(act, probs_turned, at(j, 1, 1))
                A(prob_t[:].rearrange("p n t -> p (n t)"), pw[:, 0:3, :].rearrange("p b n -> p (b n)"),
                  ACT.Copy).then_inc(probs_copied, 1)

            def att_hi(j):
                wait(act, att_turned, at(j, 1, 1))
                A(yatt_hl[:, ds(j, 2, 0, 2), 0, :], pw[:, 3, :].rearrange("p (f t) -> p f t", f=2),
                  ACT.Copy).then_inc(yatt_hi_done, 1)

            def attention(j, first=False):
                c, b = at(j, C_ATT, 8), at(j, B_ATT, 2)
                for u in range(8):
                    split(c + u)
                    if u == 2:
                        copy_low(b + (-1), c + (-1))
                    if u == 3 and not first:
                        att_exp(j - 1)
                    if u == 5 and not first:
                        att_copy_probs(j - 1)
                    if u == 6:
                        copy_low(b, c + 3)
                        if first:
                            act.wait_ge(v_turned, 1)
                            A(v_tm[:], pw[:, 0:2, :], ACT.Copy).then_inc(v_ready, 1)
                    if u == 7 and not first:
                        att_hi(j - 1)

            attention(0, first=True)
            with act.Fori(1, KV_HEADS) as j:
                attention(j)

            tail = KV_HEADS - 1

            def gate_sigmoid(i, n, branch, evacuated, done):
                act.wait_ge(block_evacuated, evacuated)
                v = gates[:, ds(i * 2, 2, 2 * n, 2), branch, :]
                A(v, v, ACT.Sigmoid).then_inc(done, 1)

            def pb_block(i, n, extra=None):
                c, b, prev_last = at(i, C_PB + 4 * n, 8), at(i, B_PB + n, 2), at(i, C_PB + 4 * n - 1, 8)
                for u in range(4):
                    split(c + u)
                    if u == 1:
                        gate_sigmoid(i, n - 1, 1, B_DT, gb_sigmoid)
                    if u == 2:
                        copy_low(b + (-1), prev_last)
                    if extra:
                        extra(u)

            split(Count(C_DT))
            split(Count(C_DT + 1))
            split(Count(C_PB))
            copy_low(Count(B_DT - 1), Count(C_DT - 1))
            split(Count(C_PB + 1))
            att_exp(tail)
            split(Count(C_PB + 2))
            copy_low(Count(B_DT), Count(C_PB - 1), pair=1)
            split(Count(C_PB + 3))
            att_copy_probs(tail)
            A(neg_a[:], hd[:, 1:2], ACT.Exp)
            act.wait_ge(dt_neg_abs, 1)
            A(dts[2][:], dts[1][:], ACT.Exp).then_inc(dt_exp, 1)
            split(Count(C_PB + 4))
            split(Count(C_PB + 5))
            att_hi(tail)
            split(Count(C_PB + 6))
            copy_low(Count(B_PB), Count(C_PB + 3))
            gate_sigmoid(0, 0, 1, B_DT, gb_sigmoid)
            split(Count(C_PB + 7))
            with act.Fori(1, 3) as i:
                for n in range(2):
                    pb_block(i, n)

            def dt_early(u):
                if u == 3:
                    act.wait_ge(dt_turned, 1)
                    A(dt_tm[:].rearrange("p t h -> p (t h)"), pw[:, 0, 0:P], ACT.Copy)
                    A(da_tm[:].rearrange("p t h -> p (t h)"), pw[:, 0, P:2 * P], ACT.Copy).then_inc(dt_copied, 1)

            def dt_late(u):
                if u == 2:
                    act.wait_ge(cum_done, 1)
                    A(dts[0][:], pw[0:64, 2, 0:256], ACT.Copy).then_inc(cum_copied, 1)

            pb_block(3, 0, dt_early)
            pb_block(3, 1, dt_late)
            gate_sigmoid(3, 1, 1, B_DT, gb_sigmoid)

            def conv_silu(g, n):
                wait(act, conv_done, at(g, n + 1, 3))
                v = xc[:, 2 * n:2 * n + 2, :]
                A(v, v, ACT.Silu).then_inc(conv_silu_done, 1)

            def z_silu(g, n):
                wait(act, block_evacuated, at(g, B_SSD + 4 + n, 6))
                v = zc[:, 2 * n:2 * n + 2, :]
                A(v, v, ACT.Silu).then_inc(z_silu_done, 1)

            def ssd_decay(g, half):
                wait(act, seg_ready, at(g, half + 1, 2))
                v = weights[:, 4 * half:4 * half + 4, :]
                A(v, v, ACT.Exp).then_inc(decay_done, 1)

            def ssd_square(g):
                wait(act, gated, at(g, 1, 1))
                A(square[:], xc[:, 0:4, :], ACT.Square).then_inc(squared, 1)

            def ssd_sqrt(g):
                wait(act, var_ready, at(g, 1, 1))
                A(rstd[:], rstd[:], ACT.Sqrt).then_inc(sqrt_done, 1)

            def y_hi_part(n):
                act.wait_ge(y_ready, n + 1)
                act.wait_ge(seg_ready, 2 * SSD_GROUPS)
                o = Y_TILE[n]
                A(y_hi[:, o:o + 4, :], y_plain[:, 4 * n:4 * n + 4, :], ACT.Copy).then_inc(y_hi_done, 1)

            def ssd(g, first=False, last=False):
                c, b = at(g, C_SSD, 24), at(g, B_SSD, 6)
                for u in range(24):
                    split(c + u)
                    if u == 1 and not first:
                        ssd_square(g - 1)
                    if u == 2:
                        copy_low(b + (-1), c + (-1))
                    if u == 5 and not first:
                        ssd_sqrt(g - 1)
                    if u in (18, 19):
                        ssd_decay(g, u - 18)
                    if u in (6, 10):
                        copy_low(b + (u - 6) // 4, c + (u - 3))
                    if u in (9, 12, 15):
                        conv_silu(g, (9, 12, 15).index(u))
                    if u == 14:
                        copy_low(b + 2, c + 11)
                    if u in (18, 22):
                        copy_low(b + 3 + (u - 18) // 4, c + (u - 3))
                    if u in (22, 23):
                        z_silu(g, u - 22)
                    if last and u in (20, 21):
                        y_hi_part(u - 20)

            ssd(0, first=True)
            with act.Fori(1, SSD_GROUPS - 1) as g:
                ssd(g)
            ssd(SSD_GROUPS - 1, last=True)

            def merged_hi(i, n):
                wait(act, merged_ready, at(i, n + 1, 2))
                A(merged_hl[:, ds(i, 4, 2 * n, 2), 0, :], tmp[:], ACT.Copy).then_inc(merged_hi_done, 1)

            last = SSD_GROUPS - 1
            for u in range(8):
                split(Count(C_PA + u))
                if u == 1:
                    ssd_square(last)
                if u == 2:
                    copy_low(Count(B_PA - 1), Count(C_PA - 1))
                if u == 4:
                    ssd_sqrt(last)
                if 1 <= u <= 5:
                    y_hi_part(u + 1)
                if u == 7:
                    y_hi_part(7)

            def pa_block(i, n, first=False):
                for u in range(8):
                    split(at(i, C_PA + 8 * n + u, 16))
                    if u == 1:
                        gate_sigmoid(i, n - 1, 0, B_PA, ga_sigmoid)
                    if u == 2:
                        copy_low(at(i, B_PA + n - 1, 2), at(i, C_PA + 8 * n - 1, 16))
                    if u == 4:
                        merged_hi(i, n - 1)

            pa_block(0, 1)
            with act.Fori(1, 4) as i:
                pa_block(i, 0)
                pa_block(i, 1)

            def o_block(i, n, after_pa=False, square=False):
                for u in range(4):
                    split(at(i, C_O + 4 * n + u, 8))
                    if u == 3 and square:
                        o_square(i, n - 1)
                    if u == 1 and after_pa:
                        gate_sigmoid(3, 1, 0, B_PA, ga_sigmoid)
                    if u == 2:
                        copy_low(at(i, B_O + n - 1, 2), at(i, C_O + 4 * n - 1, 8))
                    if u == 3 and after_pa:
                        merged_hi(3, 1)

            def ln_square_first(n):
                act.wait_ge(ln_shifted, 7 * n + 1)
                A(sq4[:], res[:, 0:4, :], ACT.Square).then_inc(ln_squared, 1)

            def ln_square(count, cols):
                wait(act, ln_shifted, count)
                A(sq2[:], res[:, cols, :], ACT.Square).then_inc(ln_squared, 1)

            def o_square(i, n):
                ln_square(at(i, n, 2), ds(i * 2, 2, 2 * n, 2))

            o_block(0, 0, after_pa=True)
            o_block(0, 1)
            o_block(1, 0)
            for u in range(4):
                split(Count(C_O + 12 + u))
                if u == 1:
                    ln_square_first(0)
                if u == 2:
                    copy_low(Count(B_O + 2), Count(C_O + 11))
                if u == 3:
                    o_square(1, 0)
            with act.Fori(2, 4) as i:
                o_block(i, 0, square=True)
                o_block(i, 1, square=True)

            def layer_norm(n):
                act.wait_ge(ln_var_ready, n + 1)
                A(lrstd[:], lstat[:], ACT.Sqrt, bias=ln_eps[:]).then_inc(ln_sqrt_done, 1)
                for k in range(KT if n == 0 else KT - DVE_BIASES):
                    act.wait_ge(ln_scaled, k + 1 if n == 0 else KT + k // 4 + 1)
                    gain, bias = (par[:, LN_COL + KT * (2 * n + m) + k:LN_COL + KT * (2 * n + m) + k + 1] for m in range(2))
                    if n == 0:
                        A(x1_hl[:, k, 0, :], res[:, k, :], ACT.Identity, bias=bias).then_inc(x1_hi_done, 1)
                    else:
                        A(res[:, k, :], res[:, k, :], ACT.Identity, bias=bias, scale=gain).then_inc(out_ready, 1)

            def h_hi(i):
                wait(act, h_taken, at(i, 1, 1))
                A(h_hl[:, ds(i, 2, 0, 2), 0, :], t2[:], ACT.Copy).then_inc(h_hi_done, 1)

            def gate_up(i, first=False):
                c, b = at(i, C_GU, 8), at(i, B_GU, 2)
                for u in range(8):
                    split(c + u)
                    if u == 2:
                        copy_low(b + (-1), c + (-1))
                    if u == 3:
                        if first:
                            o_square(3, 1)
                            layer_norm(0)
                        else:
                            h_hi(i - 1)
                    if u == 6:
                        copy_low(b, c + 3)
                    if u == 7:
                        wait(act, block_evacuated, b + 1)
                        A(gate_g[:], gate_g[:], ACT.Silu).then_inc(gate_silu, 1)

            gate_up(0, first=True)
            with act.Fori(1, GU_PAIRS) as i:
                gate_up(i)

            def down_square(i, n):
                ln_square(at(i, 7 + n, 4), ds(i * 4, 2, 2 * n, 2))

            def down(i, first=False):
                for n in range(4):
                    c, b = at(i, C_DN + 11 * n, 44), at(i, B_DN + n, 4)
                    for u in range(11):
                        split(c + u)
                        if u == 2:
                            copy_low(b + (-1), c + (-1))
                        if u == 3:
                            if n == 0 and first:
                                h_hi(GU_PAIRS - 1)
                            if n == 3 or not first:
                                down_square(i, n - 1)
                        if u == 1 and n == 3 and first:
                            ln_square_first(1)

            down(0, first=True)
            with act.Fori(1, 2) as i:
                down(i)
            copy_low(Count(B_DN + 7), Count(C_DN + 87))
            down_square(1, 3)
            layer_norm(1)

        @block.vector
        def _(dve):
            V = nc.vector
            chain = Chain(dve, dve_step)

            def split(c):
                slot = c.base % RING
                wait(dve, hi_split, c + 1)
                V.tensor_tensor(w_lo[:, slot, :], raw[:, slot, :], w_hi[:, slot, :].bitcast(F32),
                                ALU.subtract).then_inc(lo_split, 1)

            def take(b, out, pair=2, rows=P):
                wait(dve, low_copied, b + 1)
                p_ = b.base % 2
                src, lo = ps[0:rows, 2 * p_:2 * p_ + pair, 0, :], low[0:rows, p_, 0:pair, :]
                V.tensor_tensor(out, src, lo, ALU.add).then_inc(block_evacuated, 1)

            def taken(b):
                wait(dve, block_evacuated, b + 1)

            V.memset(ln_eps[:], LN_EPS)
            V.memset(kz[:], 0.0).then_inc(dve_step, 1)
            chain.total += 1
            for c in range(16):
                if c < 4:
                    dve.wait_ge(x_hi_done, c + 1)
                    V.tensor_tensor(x_hl[:, 4 * c:4 * c + 4, 1, :], x_raw[:, 4 * c:4 * c + 4, :],
                                    x_hl[:, 4 * c:4 * c + 4, 0, :].bitcast(F32), ALU.subtract).then_inc(x_lo_done, 1)
                split(Count(c))
                if c >= 6 and c % 4 == 2:
                    n = (c - 6) // 4
                    take(Count(n), kv_fm[:, 2 * n:2 * n + 2, :])
            dve.wait_ge(consts_landed, 64)

            def over(v, n):
                return v.unsqueeze(2).to_broadcast([P, 4, n])

            def sink(j):
                return sink_b[:, ds(j, 4, 0, 4)]

            halves = [prob[:, :, 0:P], prob[:, :, P:384]]

            def att_mask(j):
                wait(dve, scores_done, at(j, 1, 1))
                V.scalar_tensor_tensor(halves[0], pw[:, 0, :].rearrange("p (h s) -> p h s", h=4), ATT_SCALE,
                                       band[:, 0:P].unsqueeze(1).to_broadcast([P, 4, P]), ALU.mult, ALU.add)
                for n in range(2):
                    ins = V.scalar_tensor_tensor(prob[:, 2 * n:2 * n + 2, P:384],
                                                 pw[:, 1 + n, :].rearrange("p (h s) -> p h s", h=2), ATT_SCALE,
                                                 band[:, P:384].unsqueeze(1).to_broadcast([P, 2, 256]), ALU.mult, ALU.add)
                chain.link(ins)

            def att_peak(j):
                for t in range(2):
                    ins = V.tensor_reduce(peak[:, t, :], halves[t], AX.X, ALU.max)
                chain.link(ins)
                for t in range(2):
                    ins = V.tensor_tensor(peak[:, t, :], peak[:, t, :], sink(j), ALU.max)
                chain.link(ins)

            def att_shift(j):
                for t in range(2):
                    V.tensor_tensor(halves[t], halves[t], over(peak[:, t, :], P * (t + 1)), ALU.subtract)
                V.tensor_tensor(sink_d[:, 0, :], sink(j), peak[:, 0, :], ALU.subtract)
                V.tensor_tensor(sink_d[:, 1, :], sink(j), peak[:, 1, :], ALU.subtract).then_inc(shifted, 1)

            def att_denominator(j):
                wait(dve, exp_done, at(j, 1, 1))
                for t in range(2):
                    ins = V.tensor_reduce(denom[:, t, :], halves[t], AX.X, ALU.add)
                chain.link(ins)
                chain.link(V.tensor_tensor(denom[:], denom[:], sink_d[:], ALU.add))
                chain.link(V.reciprocal(recip[:], denom[:]))

            def att_scale_out(j):
                wait(dve, att_done, at(j, 1, 1))
                V.tensor_tensor(o_tm[:], pw[:, 3, :].rearrange("p (h d) -> p h d", h=8),
                                recip[:].rearrange("p t h -> p (t h)").unsqueeze(2).to_broadcast([P, 8, ATT_HEAD_DIM]),
                                ALU.mult).then_inc(att_scaled, 1)

            def att_lo(j):
                wait(dve, yatt_hi_done, at(j, 1, 1))
                V.tensor_tensor(yatt_hl[:, ds(j, 2, 0, 2), 1, :], pw[:, 3, :].rearrange("p (f t) -> p f t", f=2),
                                yatt_hl[:, ds(j, 2, 0, 2), 0, :].bitcast(F32), ALU.subtract).then_inc(yatt_lo_done, 1)

            def pick_k(j):
                V.tensor_copy(kz[0:64, 0, :], kd[0:64, ds(j, 1, 0, 1), :].rearrange("p a t -> p (a t)"))
                V.tensor_copy(kz[64:128, 1, :], kd[64:128, ds(j, 1, 0, 1), :].rearrange("p a t -> p (a t)")
                              ).then_inc(k_picked, 1)

            def attention(j, first=False):
                c, b = at(j, C_ATT, 8), at(j, B_ATT, 2)
                for u in range(8):
                    split(c + u)
                    if not first:
                        if u == 0:
                            att_mask(j - 1)
                        if u == 1:
                            att_peak(j - 1)
                        if u == 2:
                            att_shift(j - 1)
                            take(b + (-1), gates[:, ds(j, 2, -2, 2), 1, :])
                        if u == 4:
                            att_denominator(j - 1)
                        if u == 6:
                            att_scale_out(j - 1)
                        if u == 7:
                            att_lo(j - 1)
                    elif u == 2:
                        take(b + (-1), kv_fm[:, 6:8, :])
                    if u == 6:
                        take(b, q_fm[:])
                        if first:
                            dve.wait_ge(k_spread, 64)
                        pick_k(j)
                    if u == 7:
                        if first:
                            dve.wait_ge(v_ready, 1)
                        V.tensor_copy(v_cur[:], v_tm[:, :, ds(j, ATT_HEAD_DIM, 0, ATT_HEAD_DIM)]).then_inc(v_picked, 1)

            attention(0, first=True)
            with dve.Fori(1, KV_HEADS) as j:
                chain.enter(j, 1, 6)
                attention(j)
            chain.leave(KV_HEADS - 1)

            def pb_take(i, n):
                cols = ds(i, 4, 2 * n, 2)
                b = at(i, B_PB + n, 2)
                take(b, tmp[:])
                taken(b)
                wait(dve, gb_sigmoid, at(i, n + 1, 2))
                V.tensor_tensor(gates[:, cols, 1, :], gates[:, cols, 1, :], tmp[:], ALU.mult)

            def softplus_exponent():
                taken(Count(B_DT))
                chain.link(V.tensor_scalar(dts[0][:], dts[0][:], hd[:, 0:1], None, ALU.add))
                chain.link(V.tensor_scalar(dts[1][:], dts[0][:], -1.0, None, ALU.mult))
                V.tensor_tensor(dts[1][:], dts[1][:], dts[0][:], ALU.min).then_inc(dt_neg_abs, 1)

            e, s, s2, p = dts[2], dts[3], dts[4], dts[1]

            def softplus_argument():
                dve.wait_ge(dt_exp, 1)
                chain.link(V.tensor_scalar(s[:], e[:], 2.0, None, ALU.add))
                chain.link(V.reciprocal(s[:], s[:]))
                chain.link(V.tensor_tensor(s[:], s[:], e[:], ALU.mult))
                chain.link(V.tensor_tensor(s2[:], s[:], s[:], ALU.mult))
                chain.link(V.tensor_scalar(p[:], s2[:], 1.0 / 15, None, ALU.mult))

            def softplus_terms(odds):
                for odd in odds:
                    chain.link(V.scalar_tensor_tensor(p[:], p[:], 1.0 / odd, s2[:], ALU.add, ALU.mult))

            def step_sizes():
                chain.link(V.scalar_tensor_tensor(p[:], p[:], 1.0, s[:], ALU.add, ALU.mult))
                chain.link(V.tensor_scalar(dts[0][:], dts[0][:], 0.0, None, ALU.max))
                chain.link(V.scalar_tensor_tensor(dts[5][:], p[:], 2.0, dts[0][:], ALU.mult, ALU.add))
                V.tensor_scalar(dts[6][:], dts[5][:], neg_a[:], -1.0, ALU.mult, ALU.mult).then_inc(dt_ready, 1)

            tail = KV_HEADS - 1
            split(Count(C_DT))
            att_mask(tail)
            split(Count(C_DT + 1))
            att_peak(tail)
            split(Count(C_PB))
            take(Count(B_DT - 1), gates[:, 14:16, 1, :])
            att_shift(tail)
            split(Count(C_PB + 1))
            split(Count(C_PB + 2))
            att_denominator(tail)
            take(Count(B_DT), dts[0][:].unsqueeze(1), pair=1, rows=SSD_HEADS)
            softplus_exponent()
            split(Count(C_PB + 3))
            split(Count(C_PB + 4))
            att_scale_out(tail)
            split(Count(C_PB + 5))
            att_lo(tail)
            split(Count(C_PB + 6))
            pb_take(0, 0)
            split(Count(C_PB + 7))
            softplus_argument()

            def pb_block(i, n, extra=None):
                for u in range(4):
                    split(at(i, C_PB + 4 * n + u, 8))
                    if u == 2:
                        pb_take(i, n - 1)
                    if extra:
                        extra(u)

            pieces = {0: (13, 11), 1: (9, 7), 3: (5, 3)}
            pb_block(1, 0, lambda u: softplus_terms(pieces[u]) if u in pieces else None)
            pb_block(1, 1, lambda u: step_sizes() if u == 0 else None)
            with dve.Fori(2, 3) as i:
                for n in range(2):
                    pb_block(i, n)

            def negate_sums(u):
                if u == 2:
                    dve.wait_ge(cum_done, 1)
                    chain.link(V.tensor_scalar(ncum[:].rearrange("p t h -> p (t h)"), pw[:, 1, 0:P], -1.0, None, ALU.mult))

            pb_block(3, 0)
            pb_block(3, 1, negate_sums)

            V.memset(conv_in[:], 0.0).then_inc(dve_step, 1)
            chain.total += 1
            chain.wait()

            def pick_cum(g):
                chain.link(V.tensor_copy(ncum_g[:], ncum[:, :, ds(g, HEADS_PER_GROUP, 0, HEADS_PER_GROUP)]))

            def ssd_pick(g):
                wait(dve, y_ready, at(g, 0, 1))
                V.tensor_copy(dt_g[:], dt_tm[:, :, ds(g, HEADS_PER_GROUP, 0, HEADS_PER_GROUP)])
                chain.link(V.tensor_copy(gp[:], par[:, ds(g, GP_WIDTH, 0, GP_WIDTH)]))

            def ssd_seg(g, half):
                wait(dve, c_row_landed, at(g, 16, 16))
                for h in range(4 * half, 4 * half + 4):
                    V.tensor_scalar(weights[:, h, 0:256], c_row[:, h, :], ncum_g[:, 0, h:h + 1], 0.0, ALU.add, ALU.min)
                    ins = V.tensor_scalar(weights[:, h, 256:384], c_row[:, h, P:2 * P], ncum_g[:, 1, h:h + 1], 0.0,
                                          ALU.add, ALU.min)
                ins.then_inc(seg_ready, 1)

            def conv(g, n):
                taken(at(g, B_SSD + n, 6))
                for k in range(CONV_TAPS):
                    for m in range(2):
                        f = 2 * n + m
                        w = gp[:, GP_CONV + 4 * f + k:GP_CONV + 4 * f + k + 1]
                        out, src = xc[:, f, :], conv_in[:, m, k:k + SEQ]
                        if k == 0:
                            ins = V.tensor_scalar(out, src, w, gp[:, GP_BIAS + f:GP_BIAS + f + 1], ALU.mult, ALU.add)
                        else:
                            ins = V.scalar_tensor_tensor(out, src, w, out, ALU.mult, ALU.add)
                    if k < CONV_TAPS - 1:
                        chain.link(ins)
                ins.then_inc(conv_done, 1)

            def ssd_x_dt(g):
                wait(dve, xt_done, at(g, 1, 1))
                for t in range(2):
                    V.tensor_tensor(x_dt[:, t, :].rearrange("p (h d) -> p h d", d=SSD_HEAD_DIM),
                                    pw[:, t, :].rearrange("p (h d) -> p h d", d=SSD_HEAD_DIM),
                                    dt_g[:, t, :].unsqueeze(2).to_broadcast([P, HEADS_PER_GROUP, SSD_HEAD_DIM]),
                                    ALU.mult).then_inc(x_dt_ready, 1)
                chain.link(V.tensor_tensor(cb[:], pw[:, 2, 0:384], causal, ALU.mult))

            def ssd_weights(g, half):
                wait(dve, decay_done, at(g, half + 1, 2))
                v = weights[:, 4 * half:4 * half + 4, :]
                V.tensor_tensor(v, v, cb[:].unsqueeze(1).to_broadcast([P, 4, 384]), ALU.mult).then_inc(weights_ready, 1)

            def ssd_skip(g):
                wait(dve, y_done, at(g, 1, 1))
                for f in range(4):
                    o = 256 * (f % 2)
                    ins = V.scalar_tensor_tensor(xc[:, f, :], xc[:, f, :], gp[:, GP_SKIP + f:GP_SKIP + f + 1],
                                                 pw[:, 2 + f // 2, o:o + 256], ALU.mult, ALU.add)
                chain.link(ins)

            def ssd_gate(g):
                wait(dve, z_silu_done, at(g, 2, 2))
                V.tensor_tensor(xc[:, 0:4, :], xc[:, 0:4, :], zc[:], ALU.mult).then_inc(gated, 1)

            def ssd_square_sum(g):
                wait(dve, squared, at(g, 1, 1))
                V.tensor_reduce(stat[:], square[:].rearrange("p f t -> p t f"), AX.X, ALU.add).then_inc(square_summed, 1)

            def ssd_var(g):
                wait(dve, norm_summed, at(g, 1, 1))
                V.tensor_scalar(rstd[:], pw[:, 0, 0:256], float(SSD_GROUPS) / SSD_INNER, RMS_EPS,
                                ALU.mult, ALU.add).then_inc(var_ready, 1)

            def ssd_rstd(g):
                wait(dve, sqrt_done, at(g, 1, 1))
                chain.link(V.reciprocal(rstd[:], rstd[:]))

            def ssd_out(g):
                wait(dve, gated, at(g, 1, 1))
                for f in range(4):
                    ins = V.scalar_tensor_tensor(y_plain[:, ds(g, 4, f, 1), :].rearrange("p a t -> p (a t)"), xc[:, f, :],
                                                 gp[:, GP_NORM + f:GP_NORM + f + 1], rstd[:], ALU.mult, ALU.mult)
                ins.then_inc(y_ready, 1)

            def y_lo_part(n):
                dve.wait_ge(y_hi_done, n + 1)
                o = Y_TILE[n]
                V.tensor_tensor(y_lo[:, 4 * n:4 * n + 4, :], y_plain[:, 4 * n:4 * n + 4, :],
                                y_hi[:, o:o + 4, :].bitcast(F32), ALU.subtract).then_inc(y_lo_done, 1)

            def ssd(g, first=False, last=False):
                c, b = at(g, C_SSD, 24), at(g, B_SSD, 6)
                conv_cols = conv_in[:, :, CONV_TAPS - 1:CONV_TAPS - 1 + SEQ]
                for u in range(24):
                    split(c + u)
                    if not first:
                        if u == 0:
                            ssd_skip(g - 1)
                        if u == 1:
                            ssd_gate(g - 1)
                        if u == 2:
                            ssd_square_sum(g - 1)
                            take(b + (-1), gates[:, ds(g, 2, -2, 2), 0, :])
                        if u == 5:
                            ssd_var(g - 1)
                        if u == 6:
                            ssd_rstd(g - 1)
                        if u == 7:
                            ssd_out(g - 1)
                    elif u == 2:
                        pb_take(3, 1)
                    if u == 7:
                        ssd_pick(g)
                    if u in (6, 10):
                        take(b + (u - 6) // 4, conv_cols)
                    if u in (8, 11):
                        conv(g, (8, 11).index(u))
                    if u == 14:
                        take(b + 2, conv_cols)
                        conv(g, 2)
                    if u == 16:
                        pick_cum(g)
                    if u in (16, 17):
                        ssd_seg(g, u - 16)
                    if u == 18:
                        take(b + 3, zc[:, 0:2, :])
                        ssd_x_dt(g)
                    if u in (20, 21):
                        ssd_weights(g, u - 20)
                    if u == 22:
                        take(b + 4, zc[:, 2:4, :])
                    if last and u in (22, 23):
                        y_lo_part(u - 22)

            ssd(0, first=True)
            with dve.Fori(1, SSD_GROUPS - 1) as g:
                chain.enter(g, 1, 14)
                ssd(g)
            chain.leave(SSD_GROUPS - 2)
            ssd(SSD_GROUPS - 1, last=True)

            def pa_take(i, n):
                cols = ds(i, 4, 2 * n, 2)
                b = at(i, B_PA + n, 2)
                take(b, tmp[:])
                taken(b)
                wait(dve, ga_sigmoid, at(i, n + 1, 2))
                chain.link(V.tensor_tensor(tmp[:], tmp[:], gates[:, cols, 0, :], ALU.mult))
                V.tensor_tensor(tmp[:], tmp[:], gates[:, cols, 1, :], ALU.add).then_inc(merged_ready, 1)

            def merged_lo(i, n):
                cols = ds(i, 4, 2 * n, 2)
                wait(dve, merged_hi_done, at(i, n + 1, 2))
                V.tensor_tensor(merged_hl[:, cols, 1, :], tmp[:], merged_hl[:, cols, 0, :].bitcast(F32),
                                ALU.subtract).then_inc(merged_lo_done, 1)

            last = SSD_GROUPS - 1
            for u in range(8):
                split(Count(C_PA + u))
                if u == 0:
                    ssd_skip(last)
                if u == 1:
                    ssd_gate(last)
                if u == 2:
                    ssd_square_sum(last)
                    take(Count(B_PA - 1), gates[:, 2 * last:2 * last + 2, 0, :])
                if u == 4:
                    ssd_var(last)
                if u == 5:
                    ssd_rstd(last)
                if u == 6:
                    ssd_out(last)
                if 1 <= u <= 5:
                    y_lo_part(u + 1)
                if u == 7:
                    y_lo_part(7)

            def pa_block(i, n):
                for u in range(8):
                    split(at(i, C_PA + 8 * n + u, 16))
                    if u == 2:
                        pa_take(i, n - 1)
                    if u == 5:
                        merged_lo(i, n - 1)

            pa_block(0, 1)
            with dve.Fori(1, 4) as i:
                chain.enter(i, 1, 2)
                pa_block(i, 0)
                pa_block(i, 1)
            chain.leave(3)

            def first_residual(b, cols, x, start, done=None):
                take(b, t2[:])
                taken(b)
                r = res[:, cols, :]
                chain.link(V.scalar_tensor_tensor(r, x[:, cols, 0, :].bitcast(F32), ALPHA, t2[:], ALU.mult, ALU.add))
                chain.link(V.scalar_tensor_tensor(r, x[:, cols, 1, :].bitcast(F32), ALPHA, r, ALU.mult, ALU.add))
                if start:
                    chain.link(V.tensor_tensor(acc[:, 0, :], res[:, 0, :], res[:, 1, :], ALU.add))
                else:
                    chain.link(V.tensor_tensor(acc[:, 0, :], acc[:, 0, :], res[:, 2, :], ALU.add))
                    V.tensor_tensor(acc[:, 0, :], acc[:, 0, :], res[:, 3, :], ALU.add).then_inc(ln_acc_ready, 1)

            def over2(v):
                return v[:].unsqueeze(1).to_broadcast([P, 2, SEQ])

            def over4(v):
                return v[:].unsqueeze(1).to_broadcast([P, 4, SEQ])

            def ln_shift(n):
                dve.wait_ge(ln_summed, 2 * n + 1)
                chain.link(V.tensor_scalar(shift[:], pw[:, 0, 0:256], 1.0 / (4 * P), None, ALU.mult))
                V.tensor_tensor(res[:, 0:4, :], res[:, 0:4, :], over4(shift), ALU.subtract).then_inc(ln_shifted, 1)

                dve.wait_ge(ln_shifted, 7 * n + 1)
                chain.link(V.tensor_reduce(acc[:, 0, :], res[:, 0:4, :].rearrange("p f t -> p t f"), AX.X, ALU.add))

            def ln_first_squares(n):
                dve.wait_ge(ln_squared, 7 * n + 1)
                chain.link(V.tensor_reduce(acc[:, 1, :], sq4[:].rearrange("p f t -> p t f"), AX.X, ALU.add))

            def x_part(cols, x):
                chain.link(V.scalar_tensor_tensor(x_term[:], x[:, cols, 0, :].bitcast(F32), ALPHA, over2(shift),
                                                  ALU.mult, ALU.subtract))
                chain.link(V.scalar_tensor_tensor(x_term[:], x[:, cols, 1, :].bitcast(F32), ALPHA, x_term[:],
                                                  ALU.mult, ALU.add))

            def tile_of(buf, i, step, base):
                return buf[:, ds(i, step, base, 1), :].rearrange("p a t -> p (a t)")

            def add_tiles(into, tiles, done):
                chain.link(V.tensor_tensor(into, into, tiles[0], ALU.add))
                ins = V.tensor_tensor(into, into, tiles[1], ALU.add)
                if done is not None:
                    ins.then_inc(done, 1)
                else:
                    chain.link(ins)

            def next_residual(b, i, step, base, count, done=None):
                take(b, t2[:])
                taken(b)
                V.tensor_tensor(res[:, ds(i, step, base, 2), :], t2[:], x_term[:], ALU.add).then_inc(ln_shifted, 1)
                wait(dve, ln_shifted, count)
                add_tiles(acc[:, 0, :], [tile_of(res, i, step, base + m) for m in range(2)], done)

            def add_squares(count, done=None):
                wait(dve, ln_squared, count)
                add_tiles(acc[:, 1, :], [sq2[:, m, :] for m in range(2)], done)

            def o_step(u, i, n, start=False, last=False):
                if u == 1:
                    x_part(ds(i, 4, 2 * n, 2), x_hl)
                if u == 2:
                    if start:
                        ln_first_squares(0)
                    next_residual(at(i, B_O + n, 2), i, 4, 2 * n, at(i, n, 2), ln_acc_ready if last else None)
                if u == 3:
                    add_squares(at(i, n, 2), ln_sq_ready if last else None)

            for u in range(4):
                split(Count(C_O + u))
                if u == 2:
                    pa_take(3, 1)
                if u == 3:
                    merged_lo(3, 1)
            for b in (1, 2):
                for u in range(4):
                    split(Count(C_O + 4 * b + u))
                    if u == 2:
                        first_residual(Count(B_O + b - 1), slice(2 * b - 2, 2 * b), x_hl, b == 1)
            for u in range(4):
                split(Count(C_O + 12 + u))
                if u == 1:
                    ln_shift(0)
                o_step(u, 1, 0, start=True)
            with dve.Fori(2, 4) as i:
                chain.enter(i, 2, 12)
                for n in range(2):
                    for u in range(4):
                        split(at(i, C_O + 4 * n + u, 8))
                        o_step(u, i, n - 1)
            chain.leave(2)

            def layer_norm(n):
                def centre(k, tiles=4):
                    r = res[:, k:k + tiles, :]
                    chain.link(V.tensor_tensor(r, r, delta[:].unsqueeze(1).to_broadcast([P, tiles, SEQ]), ALU.subtract))

                dve.wait_ge(ln_summed, 2 * n + 2)
                chain.link(V.tensor_scalar(delta[:], pw[:, 0, 0:256], 1.0 / D_MODEL, None, ALU.mult))
                chain.link(V.tensor_tensor(delta_sq[:], delta[:], delta[:], ALU.mult))
                dve.wait_ge(ln_sq_summed, n + 1)
                V.scalar_tensor_tensor(lstat[:], pw[:, 1, 0:256], 1.0 / D_MODEL, delta_sq[:], ALU.mult, ALU.subtract
                                       ).then_inc(ln_var_ready, 1)
                centre(0, 2)
                dve.wait_ge(ln_sqrt_done, n + 1)
                chain.link(V.reciprocal(lrstd[:], lrstd[:]))

                def x1_lo(k):
                    dve.wait_ge(x1_hi_done, k + 1)
                    bias = par[:, LN_COL + KT + k:LN_COL + KT + k + 1]
                    V.scalar_tensor_tensor(x1_hl[:, k, 1, :], res[:, k, :], bias, x1_hl[:, k, 0, :].bitcast(F32),
                                           ALU.add, ALU.subtract).then_inc(x1_lo_done, 1)

                if n == 0:
                    for k in range(KT):
                        if k == 2:
                            centre(2, 2)
                        if k % 4 == 0 and k > 0:
                            centre(k)
                        gain = par[:, LN_COL + k:LN_COL + k + 1]
                        V.scalar_tensor_tensor(res[:, k, :], res[:, k, :], gain, lrstd[:], ALU.mult, ALU.mult
                                               ).then_inc(ln_scaled, 1)
                        if k % 4 >= 2:
                            x1_lo(k - 2)
                        if k % 4 == 3:
                            x1_lo(k - 1)
                            x1_lo(k)
                        if k in (7, 11):
                            split(Count(C_GU + 2 + k // 8))
                else:
                    centre(2, 2)
                    for k in range(0, KT, 4):
                        if k > 0:
                            centre(k)
                        r = res[:, k:k + 4, :]
                        V.tensor_tensor(r, r, over4(lrstd), ALU.mult).then_inc(ln_scaled, 1)
                    dve.wait_ge(ln_scaled, KT + 4)
                    for k in range(KT - DVE_BIASES, KT):
                        gain, bias = (par[:, LN_COL + KT * m + k:LN_COL + KT * m + k + 1] for m in (2, 3))
                        V.tensor_scalar(res[:, k, :], res[:, k, :], gain, bias, ALU.mult, ALU.add).then_inc(out_ready_dve, 1)

            def up_take(i):
                b = at(i, B_GU + 1, 2)
                take(b, t2[:])
                wait(dve, gate_silu, at(i, 1, 1))
                taken(b)
                V.tensor_tensor(t2[:], t2[:], gate_g[:], ALU.mult).then_inc(h_taken, 1)

            def h_lo(i):
                wait(dve, h_hi_done, at(i, 1, 1))
                cols = ds(i, 2, 0, 2)
                V.tensor_tensor(h_hl[:, cols, 1, :], t2[:], h_hl[:, cols, 0, :].bitcast(F32), ALU.subtract
                                ).then_inc(h_lo_done, 1)

            def gate_up(i, first=False):
                c, b = at(i, C_GU, 8), at(i, B_GU, 2)
                if first:
                    o_step(1, 3, 1)
                for u in range(8):
                    if u == 2 and first:
                        o_step(2, 3, 1, last=True)
                        o_step(3, 3, 1, last=True)
                        layer_norm(0)
                        continue
                    if u == 3 and first:
                        continue
                    split(c + u)
                    if u == 2 and not first:
                        up_take(i - 1)
                    if u == 4 and not first:
                        h_lo(i - 1)
                    if u == 6:
                        take(b, gate_g[:])

            gate_up(0, first=True)
            with dve.Fori(1, GU_PAIRS) as i:
                gate_up(i)

            def down_step(u, i, n, start=False, last=False):
                if u == 1:
                    x_part(ds(i, 8, 2 * n, 2), x1_hl)
                if u == 2:
                    if start:
                        ln_first_squares(1)
                    next_residual(at(i, B_DN + n, 4), i, 8, 2 * n, at(i, 7 + n, 4), ln_acc_ready if last else None)
                if u == 3:
                    add_squares(at(i, 7 + n, 4), ln_sq_ready if last else None)

            def down(i, first=False):
                for n in range(4):
                    for u in range(11):
                        split(at(i, C_DN + 11 * n + u, 44))
                        if not first:
                            down_step(u, i, n - 1)
                            continue
                        if n == 0 and u == 2:
                            up_take(GU_PAIRS - 1)
                        if n == 0 and u == 4:
                            h_lo(GU_PAIRS - 1)
                        if n in (1, 2) and u == 2:
                            first_residual(Count(B_DN + n - 1), slice(2 * n - 2, 2 * n), x1_hl, n == 1)
                        if n == 3:
                            if u == 1:
                                ln_shift(1)
                            down_step(u, 0, 2, start=True)

            down(0, first=True)
            with dve.Fori(1, 2) as i:
                chain.enter(i, 1, 24)
                down(i)
            chain.leave(1)
            down_step(1, 1, 3)
            down_step(2, 1, 3, last=True)
            down_step(3, 1, 3, last=True)
            layer_norm(1)


def constants():
    r = np.arange(P)
    cst = np.zeros((P, K_WIDTH), np.float32)
    cst[:, K_ID:K_ID + P] = np.eye(P)
    cst[:, K_ONES:K_ONES + P] = 1.0
    s, l = r[:, None], r[None, :]
    cst[:, K_CUM0:K_CUM0 + P] = -(s > l).astype(np.float32)
    cst[:, K_CUM1:K_CUM1 + P] = s <= l
    cst[:, K_CAUSAL:K_CAUSAL + P] = s <= l
    cst[:, K_CAUSAL + P:K_CAUSAL + 2 * P] = 1.0
    cst[:, K_CAUSAL + 2 * P:K_CAUSAL + 3 * P] = s <= l
    for t in range(2):
        q = (r + P * t)[:, None] // ATT_CHUNK
        k = np.arange(P * (t + 1))[None, :] // ATT_CHUNK
        o = K_BAND + (0 if t == 0 else P)
        cst[:, o:o + P * (t + 1)] = np.where((k == q) | (k == q - 1), 0.0, -1e30)
    return cst


def kernel(**inputs):
    import concourse.bacc as bacc
    from concourse.bass_utils import run_bass_kernel_spmd

    a = {n: np.asarray(v) for n, v in inputs.items()}

    def tiles(v):
        return v.reshape(-1, P).T

    groups = []
    for g in range(SSD_GROUPS):
        feats = [4 * g, 4 * g + 1, 4 * g + 2, 4 * g + 3, KT_Y + g, KT_Y + SSD_GROUPS + g]
        conv = a["conv_w"][0].reshape(CONV_TAPS, -1, P)[:, feats]
        groups.append(conv.transpose(2, 1, 0).reshape(P, -1))
        groups.append(tiles(a["conv_b"][0])[:, feats])
        groups.append(tiles(np.repeat(a["d_skip"][0], SSD_HEAD_DIM))[:, 4 * g:4 * g + 4])
        groups.append(tiles(a["ssd_norm_w"][0])[:, 4 * g:4 * g + 4])
    norms = [tiles(a[n][0]) for n in ("ln1_g", "ln1_b", "ln2_g", "ln2_b")]
    arrays = {
        "x_t": a["x"][0].T,
        "w_in": a["w_in"][0],
        "heads": np.stack([a["dt_bias"][0], a["a_log"][0]], axis=1),
        "sinks": a["sinks"],
        "w_pa": a["w_pa"][0],
        "w_pb": a["w_pb"][0],
        "w_o": a["w_o"][0],
        "w_gu": a["w_gu"][0],
        "w_down": a["w_down"][0],
        "consts": constants(),
        "params": np.concatenate(groups + norms, axis=1),
    }
    nc = bacc.Bacc("TRN2", target_bir_lowering=False, num_devices=1)
    args = []
    for name in arrays:
        arrays[name] = np.ascontiguousarray(arrays[name])
        args.append(nc.dram_tensor(name, arrays[name].shape, mybir.dt.from_np(arrays[name].dtype), kind="ExternalInput").ap())
    out = nc.dram_tensor("out_t", (D_MODEL, SEQ), F32, kind="ExternalOutput").ap()
    hybrid_trunk(nc, *args, out)
    got = run_bass_kernel_spmd(nc, [arrays], core_ids=[0])
    return np.ascontiguousarray(got.results[0]["out_t"].T)[None]
```
